# Optimizing a Trainium2 kernel written in Bass

```python
import math, functools
import jax, jax.numpy as jnp
from jax import lax
import numpy as np
import math

D_MODEL = 1024
BATCH = 1
SEQ = 512
DEPTH = 1

N_HEADS_A = 8
HEAD_DIM = 64
N_KV_GROUPS = 2
Q_PER_GROUP = N_HEADS_A // N_KV_GROUPS
D_ATTN = N_HEADS_A * HEAD_DIM
D_KV = N_KV_GROUPS * HEAD_DIM
CMP_BLOCK = 32
CMP_STRIDE = 16
CMP_HIDDEN = 256
SLC_BLOCK = 64
N_SELECT = 16
N_LOCAL = 2
WINDOW = 512
Q_CHUNK = 128
ATTN_SCALE = HEAD_DIM ** -0.5
NEG = -1e30
FORCE_SCORE = 1e4
D_RNN = D_MODEL
N_RNN_BLOCKS = 16
RNN_BLOCK = D_RNN // N_RNN_BLOCKS
CONV_WIDTH = 4
LRU_C = 8.0
D_FF = 4 * D_MODEL
EPS = 1e-6

IN_SIZES = (D_ATTN, D_KV, D_KV, D_KV, D_KV, D_KV, D_KV, N_HEADS_A * 3, D_RNN, D_RNN, D_MODEL, D_MODEL)
IN_SPLITS = tuple(int(v) for v in np.cumsum(IN_SIZES)[:-1])
D_IN = int(sum(IN_SIZES))


def rms_norm(x, w):
    xf = x.astype(jnp.float32)
    var = jnp.mean(xf * xf, axis=-1, keepdims=True)
    return (xf * lax.rsqrt(var + EPS) * w.astype(jnp.float32)).astype(x.dtype)

def masked_softmax(s, mask):
    s = jnp.where(mask, s.astype(jnp.float32), NEG)
    m = jnp.max(s, axis=-1, keepdims=True)
    e = jnp.where(mask, jnp.exp(s - m), 0.0)
    return e / jnp.maximum(jnp.sum(e, axis=-1, keepdims=True), 1e-20)

def compress_blocks(k, pos, w1, w2):
    B, S = k.shape[0], k.shape[1]
    kb = k.reshape(B, S // CMP_STRIDE, CMP_STRIDE, N_KV_GROUPS, HEAD_DIM)
    blocks = jnp.concatenate([kb[:, :-1], kb[:, 1:]], axis=2) + pos[:, None, :]
    nc = blocks.shape[1]
    flat = blocks.transpose(0, 1, 3, 2, 4).reshape(B, nc, N_KV_GROUPS, CMP_BLOCK * HEAD_DIM)
    c = jax.nn.gelu(flat @ w1) @ w2
    return c.transpose(0, 2, 1, 3)

def nsa_attention(q, k_cmp, v_cmp, k_slc, v_slc, k_win, v_win, gates, pos_k, pos_v, ck_w1, ck_w2, cv_w1, cv_w2):
    B, S = q.shape[0], q.shape[1]
    G, R, dh = N_KV_GROUPS, Q_PER_GROUP, HEAD_DIM
    nb = S // SLC_BLOCK
    nc = S // CMP_STRIDE - 1
    nqb = S // Q_CHUNK
    k_sel = min(N_SELECT, nb)
    r_s = SLC_BLOCK // CMP_STRIDE
    r_c = CMP_BLOCK // CMP_STRIDE
    off = r_s + r_c - 2

    qh = q.reshape(B, S, G, R, dh).transpose(0, 2, 3, 1, 4)
    gh = gates.reshape(B, S, G, R, 3).transpose(0, 2, 3, 1, 4)
    kc = compress_blocks(k_cmp, pos_k, ck_w1, ck_w2)
    vc = compress_blocks(v_cmp, pos_v, cv_w1, cv_w2)
    ks_blk = k_slc.transpose(0, 2, 1, 3).reshape(B, G, nb, SLC_BLOCK, dh)
    vs_blk = v_slc.transpose(0, 2, 1, 3).reshape(B, G, nb, SLC_BLOCK, dh)
    pad_w = ((0, 0), (0, 0), (WINDOW, 0), (0, 0))
    kw_pad = jnp.pad(k_win.transpose(0, 2, 1, 3), pad_w)
    vw_pad = jnp.pad(v_win.transpose(0, 2, 1, 3), pad_w)
    cmp_end = jnp.arange(nc) * CMP_STRIDE + CMP_BLOCK - 1
    blk = jnp.arange(nb)
    gather = jax.vmap(jax.vmap(lambda blocks, ix: blocks[ix]))

    def chunk(qb):
        t0 = qb * Q_CHUNK
        qc = lax.dynamic_slice_in_dim(qh, t0, Q_CHUNK, axis=3)
        gc = lax.dynamic_slice_in_dim(gh, t0, Q_CHUNK, axis=3)
        tpos = t0 + jnp.arange(Q_CHUNK)
        s = jnp.einsum('bgrcd,bgnd->bgrcn', qc, kc) * ATTN_SCALE
        p_cmp = masked_softmax(s, cmp_end[None, :] <= tpos[:, None])
        o_cmp = jnp.einsum('bgrcn,bgnd->bgrcd', p_cmp, vc.astype(jnp.float32))
        ps = jnp.pad(p_cmp.sum(axis=2), ((0, 0), (0, 0), (0, 0), (off, 0)))
        imp = 0.0
        for m in range(r_s):
            for n in range(r_c):
                st = off - m - n
                imp = imp + ps[..., st:st + r_s * (nb - 1) + 1:r_s]
        cur = tpos // SLC_BLOCK
        valid_b = blk[None, :] <= cur[:, None]
        forced = (blk[None, :] == 0) | (blk[None, :] > cur[:, None] - N_LOCAL)
        score = jnp.where(valid_b, jnp.where(forced, FORCE_SCORE, imp), NEG)
        top_s, idx = lax.top_k(score, k_sel)
        sel_ok = top_s > NEG / 2
        ksel = gather(ks_blk, idx).reshape(B, G, Q_CHUNK, k_sel * SLC_BLOCK, dh)
        vsel = gather(vs_blk, idx).reshape(B, G, Q_CHUNK, k_sel * SLC_BLOCK, dh)
        kpos = idx[..., None] * SLC_BLOCK + jnp.arange(SLC_BLOCK)
        m_slc = (sel_ok[..., None] & (kpos <= tpos[:, None, None])).reshape(B, G, 1, Q_CHUNK, k_sel * SLC_BLOCK)
        s = jnp.einsum('bgrcd,bgcnd->bgrcn', qc, ksel) * ATTN_SCALE
        o_slc = jnp.einsum('bgrcn,bgcnd->bgrcd', masked_softmax(s, m_slc), vsel.astype(jnp.float32))
        kw = lax.dynamic_slice_in_dim(kw_pad, t0, Q_CHUNK + WINDOW, axis=2)
        vw = lax.dynamic_slice_in_dim(vw_pad, t0, Q_CHUNK + WINDOW, axis=2)
        kpos_w = t0 - WINDOW + jnp.arange(Q_CHUNK + WINDOW)
        diff = tpos[:, None] - kpos_w[None, :]
        m_win = (diff >= 0) & (diff < WINDOW) & (kpos_w[None, :] >= 0)
        s = jnp.einsum('bgrcd,bgnd->bgrcn', qc, kw) * ATTN_SCALE
        o_win = jnp.einsum('bgrcn,bgnd->bgrcd', masked_softmax(s, m_win), vw.astype(jnp.float32))
        out = gc[..., 0:1] * o_cmp + gc[..., 1:2] * o_slc + gc[..., 2:3] * o_win
        return out.astype(q.dtype)

    res = lax.map(chunk, jnp.arange(nqb))
    return res.transpose(1, 0, 4, 2, 3, 5).reshape(B, S, D_ATTN)

def rg_lru_branch(xr, gate, conv_w, conv_b, w_a, b_a, w_i, b_i, lam):
    B, S = xr.shape[0], xr.shape[1]
    xp = jnp.pad(xr, ((0, 0), (CONV_WIDTH - 1, 0), (0, 0)))
    xc = conv_b
    for i in range(CONV_WIDTH):
        xc = xc + xp[:, i:i + S] * conv_w[i]
    xb = xc.reshape(B, S, N_RNN_BLOCKS, RNN_BLOCK)
    r = jax.nn.sigmoid(jnp.einsum('bshi,hij->bshj', xb, w_a).reshape(B, S, D_RNN) + b_a)
    ig = jax.nn.sigmoid(jnp.einsum('bshi,hij->bshj', xb, w_i).reshape(B, S, D_RNN) + b_i)
    log_a = -LRU_C * r.astype(jnp.float32) * jax.nn.softplus(-lam.astype(jnp.float32))
    a = jnp.exp(log_a)
    bt = jnp.sqrt(-jnp.expm1(2.0 * log_a)) * (ig * xc).astype(jnp.float32)

    def combine(lhs, rhs):
        a1, b1 = lhs
        a2, b2 = rhs
        return a1 * a2, a2 * b1 + b2

    _, h = lax.associative_scan(combine, (a, bt), axis=1)
    return h.astype(xr.dtype) * jax.nn.gelu(gate)

def first_inputs(seed: int = 0) -> dict:
    key = jax.random.key(seed)
    ks = jax.random.split(key, 24)
    f32 = jnp.float32

    def nrm(k, shape, fan_in):
        return jax.random.normal(k, shape, f32) * (fan_in ** -0.5)

    a_c = jax.random.uniform(ks[17], (DEPTH, D_RNN), f32, 0.9, 0.999)
    s_l = a_c ** (1.0 / LRU_C)
    lam = jnp.log(s_l) - jnp.log1p(-s_l)
    return {
        "x": jax.random.normal(ks[0], (BATCH, SEQ, D_MODEL), f32),
        "norm1_w": 1.0 + 0.02 * jax.random.normal(ks[1], (DEPTH, D_MODEL), f32),
        "w_in": nrm(ks[2], (DEPTH, D_MODEL, D_IN), D_MODEL),
        "cmp_pos_k": 0.1 * jax.random.normal(ks[3], (DEPTH, CMP_BLOCK, HEAD_DIM), f32),
        "cmp_pos_v": 0.1 * jax.random.normal(ks[4], (DEPTH, CMP_BLOCK, HEAD_DIM), f32),
        "cmp_k_w1": nrm(ks[5], (DEPTH, CMP_BLOCK * HEAD_DIM, CMP_HIDDEN), CMP_BLOCK * HEAD_DIM),
        "cmp_k_w2": nrm(ks[6], (DEPTH, CMP_HIDDEN, HEAD_DIM), CMP_HIDDEN),
        "cmp_v_w1": nrm(ks[7], (DEPTH, CMP_BLOCK * HEAD_DIM, CMP_HIDDEN), CMP_BLOCK * HEAD_DIM),
        "cmp_v_w2": nrm(ks[8], (DEPTH, CMP_HIDDEN, HEAD_DIM), CMP_HIDDEN),
        "conv_w": nrm(ks[9], (DEPTH, CONV_WIDTH, D_RNN), CONV_WIDTH),
        "conv_b": 0.01 * jax.random.normal(ks[10], (DEPTH, D_RNN), f32),
        "lru_w_a": nrm(ks[11], (DEPTH, N_RNN_BLOCKS, RNN_BLOCK, RNN_BLOCK), RNN_BLOCK),
        "lru_b_a": 0.01 * jax.random.normal(ks[12], (DEPTH, D_RNN), f32),
        "lru_w_i": nrm(ks[13], (DEPTH, N_RNN_BLOCKS, RNN_BLOCK, RNN_BLOCK), RNN_BLOCK),
        "lru_b_i": 0.01 * jax.random.normal(ks[14], (DEPTH, D_RNN), f32),
        "lru_lambda": lam,
        "w_up_attn": nrm(ks[15], (DEPTH, D_ATTN, D_MODEL), D_ATTN),
        "w_up_rnn": nrm(ks[16], (DEPTH, D_RNN, D_MODEL), D_RNN),
        "w_out": nrm(ks[18], (DEPTH, D_MODEL, D_MODEL), D_MODEL),
        "norm2_w": 1.0 + 0.02 * jax.random.normal(ks[19], (DEPTH, D_MODEL), f32),
        "mlp_w1": nrm(ks[20], (DEPTH, D_MODEL, D_FF), D_MODEL),
        "mlp_w2": nrm(ks[21], (DEPTH, D_FF, D_MODEL), D_FF),
        "final_norm_w": 1.0 + 0.02 * jax.random.normal(ks[22], (D_MODEL,), f32),
    }

def first_block(x, norm1_w, w_in, cmp_pos_k, cmp_pos_v, cmp_k_w1, cmp_k_w2, cmp_v_w1, cmp_v_w2,
              conv_w, conv_b, lru_w_a, lru_b_a, lru_w_i, lru_b_i, lru_lambda,
              w_up_attn, w_up_rnn, w_out, norm2_w, mlp_w1, mlp_w2, final_norm_w):
    B, S = x.shape[0], x.shape[1]
    for l in range(DEPTH):
        xn = rms_norm(x, norm1_w[l])
        z = xn @ w_in[l]
        (q, k_c, v_c, k_s, v_s, k_w, v_w, g_nsa, xr, gr, g_a, g_b) = jnp.split(z, IN_SPLITS, axis=-1)
        kv_shape = (B, S, N_KV_GROUPS, HEAD_DIM)
        attn = nsa_attention(
            q.reshape(B, S, N_HEADS_A, HEAD_DIM),
            k_c.reshape(kv_shape), v_c.reshape(kv_shape),
            k_s.reshape(kv_shape), v_s.reshape(kv_shape),
            k_w.reshape(kv_shape), v_w.reshape(kv_shape),
            jax.nn.sigmoid(g_nsa).reshape(B, S, N_HEADS_A, 3),
            cmp_pos_k[l], cmp_pos_v[l], cmp_k_w1[l], cmp_k_w2[l], cmp_v_w1[l], cmp_v_w2[l])
        rnn = rg_lru_branch(xr, gr, conv_w[l], conv_b[l], lru_w_a[l], lru_b_a[l],
                            lru_w_i[l], lru_b_i[l], lru_lambda[l])
        merged = jax.nn.sigmoid(g_a) * (attn @ w_up_attn[l]) + jax.nn.sigmoid(g_b) * (rnn @ w_up_rnn[l])
        x = x + merged @ w_out[l]
        hn = rms_norm(x, norm2_w[l])
        x = x + jnp.square(jax.nn.relu(hn @ mlp_w1[l])) @ mlp_w2[l]
    return rms_norm(x, final_norm_w)


FOURIER_WIDTH = D_MODEL // 2
FOURIER_GROUPS = 4
FOURIER_GROUP_CH = FOURIER_WIDTH // FOURIER_GROUPS
SSM_WIDTH = D_MODEL // 2
SSM_GROUP_CH = 16
SSM_GROUPS = SSM_WIDTH // SSM_GROUP_CH
SSM_STATE = 64
DT_MIN = 1e-3
DT_MAX = 1e-1
N_BRANCHES = 2
IN_WIDTH = FOURIER_WIDTH + SSM_WIDTH + N_BRANCHES * D_MODEL
MOE_GROUPS = 8
EXPERTS_PER_GROUP = 8
N_EXPERTS = MOE_GROUPS * EXPERTS_PER_GROUP
MOE_TOP_K = 2
D_EXPERT = D_MODEL // 2
MOE_BLOCK = 128
RMS_EPS = 1e-6


def _rmsnorm(x, g):
    xf = x.astype(jnp.float32)
    inv = lax.rsqrt(jnp.mean(xf * xf, axis=-1, keepdims=True) + RMS_EPS)
    return (xf * inv * g.astype(jnp.float32)).astype(x.dtype)

def _fourier_mix(u):
    b, l, _ = u.shape
    ug = u.astype(jnp.float32).reshape(b, l, FOURIER_GROUPS, FOURIER_GROUP_CH)
    f = jnp.fft.fft2(ug, axes=(1, 3), norm='ortho').real
    return f.reshape(b, l, FOURIER_WIDTH).astype(u.dtype)

def _scan_combine(e1, e2):
    a1, b1 = e1
    a2, b2 = e2
    return a1 * a2, a2 * b1 + b2

def _ssm_direction(ug, a_re, a_im, log_dt, b_re, b_im, c_re, c_im, reverse):
    lam = lax.complex(a_re.astype(jnp.float32), a_im.astype(jnp.float32))
    dt = jnp.exp(log_dt.astype(jnp.float32))[:, None]
    a_bar = jnp.exp(lam * dt)
    b_mat = lax.complex(b_re.astype(jnp.float32), b_im.astype(jnp.float32))
    b_bar = ((a_bar - 1.0) / lam)[..., None] * b_mat
    bu = jnp.einsum('blgc,gnc->blgn', ug.astype(jnp.complex64), b_bar)
    a = jnp.broadcast_to(a_bar, bu.shape)
    _, h = lax.associative_scan(_scan_combine, (a, bu), axis=1, reverse=reverse)
    c_mat = lax.complex(c_re.astype(jnp.float32), c_im.astype(jnp.float32))
    return jnp.einsum('blgn,gcn->blgc', h, c_mat).real

def _ssm_mix(u, a_re, a_im, log_dt, b_re, b_im, c_re, c_im, d_skip, w_glu):
    b, l, _ = u.shape
    uf = u.astype(jnp.float32)
    ug = uf.reshape(b, l, SSM_GROUPS, SSM_GROUP_CH)
    y = (_ssm_direction(ug, a_re[0], a_im[0], log_dt[0], b_re[0], b_im[0], c_re[0], c_im[0], False)
         + _ssm_direction(ug, a_re[1], a_im[1], log_dt[1], b_re[1], b_im[1], c_re[1], c_im[1], True))
    y = y.reshape(b, l, SSM_WIDTH) + d_skip.astype(jnp.float32) * uf
    y = jax.nn.gelu(y)
    y = y * jax.nn.sigmoid(y @ w_glu.astype(jnp.float32))
    return y.astype(u.dtype)

def _hier_moe(h, wg, bg, we, be, w_gate, w_up, w_down):
    bsz, l, d = h.shape
    t = bsz * l
    ht = h.reshape(t, d)
    g_prob = jax.nn.softmax((ht @ wg).astype(jnp.float32) + bg.astype(jnp.float32), axis=-1)
    p_g, g_idx = lax.top_k(g_prob, 1)
    e_logits = ((ht @ we).astype(jnp.float32) + be.astype(jnp.float32)).reshape(t, MOE_GROUPS, EXPERTS_PER_GROUP)
    e_sel = jnp.take_along_axis(e_logits, g_idx[:, :, None], axis=1)[:, 0]
    top_l, top_i = lax.top_k(e_sel, MOE_TOP_K)
    gate_w = p_g * jax.nn.softmax(top_l, axis=-1)
    expert = g_idx * EXPERTS_PER_GROUP + top_i

    n_assign = t * MOE_TOP_K
    e_flat = expert.reshape(n_assign)
    w_flat = gate_w.reshape(n_assign)
    tok_flat = jnp.repeat(jnp.arange(t, dtype=jnp.int32), MOE_TOP_K)
    order = jnp.argsort(e_flat)
    e_s = e_flat[order]
    tok_s = tok_flat[order]
    w_s = w_flat[order]
    counts = jnp.bincount(e_flat, length=N_EXPERTS)
    starts = jnp.cumsum(counts) - counts
    padded = ((counts + MOE_BLOCK - 1) // MOE_BLOCK) * MOE_BLOCK
    pstarts = jnp.cumsum(padded) - padded
    pends = pstarts + padded
    dest = pstarts[e_s] + jnp.arange(n_assign, dtype=jnp.int32) - starts[e_s]
    n_blocks = -(-n_assign // MOE_BLOCK) + N_EXPERTS
    rows = n_blocks * MOE_BLOCK
    x_pad = jnp.zeros((rows, d), h.dtype).at[dest].set(ht[tok_s])
    block_start = jnp.arange(n_blocks, dtype=jnp.int32) * MOE_BLOCK
    block_e = jnp.minimum(jnp.searchsorted(pends, block_start, side='right'), N_EXPERTS - 1)

    def expert_block(args):
        xb, e = args
        a = jax.nn.silu(xb @ w_gate[e]) * (xb @ w_up[e])
        return a @ w_down[e]

    y_pad = lax.map(expert_block, (x_pad.reshape(n_blocks, MOE_BLOCK, d), block_e)).reshape(rows, d)
    y = y_pad[dest] * w_s[:, None].astype(h.dtype)
    out = jax.ops.segment_sum(y, tok_s, num_segments=t)
    return out.reshape(bsz, l, d)

def second_inputs(seed: int = 0) -> dict:
    key = jax.random.key(seed)
    ks = jax.random.split(key, 24)
    f32 = jnp.float32

    def nrm(k, shape, scale):
        return jax.random.normal(k, shape, f32) * scale

    S, F, D = SSM_WIDTH, FOURIER_WIDTH, D_MODEL
    G, N, C = SSM_GROUPS, SSM_STATE, SSM_GROUP_CH
    n_idx = jnp.arange(N, dtype=f32)
    return {
        'x': nrm(ks[0], (BATCH, SEQ, D), 1.0),
        'mix_norm_g': 1.0 + nrm(ks[1], (DEPTH, D), 0.02),
        'w_in': nrm(ks[2], (DEPTH, D, IN_WIDTH), D ** -0.5),
        'w_fourier_out': nrm(ks[3], (DEPTH, F, D), F ** -0.5),
        'ssm_A_re': -0.5 + nrm(ks[4], (DEPTH, 2, G, N), 0.01),
        'ssm_A_im': math.pi * n_idx + nrm(ks[5], (DEPTH, 2, G, N), 0.01),
        'ssm_log_dt': jax.random.uniform(ks[6], (DEPTH, 2, G), f32, math.log(DT_MIN), math.log(DT_MAX)),
        'ssm_B_re': nrm(ks[7], (DEPTH, 2, G, N, C), (2 * C) ** -0.5),
        'ssm_B_im': nrm(ks[8], (DEPTH, 2, G, N, C), (2 * C) ** -0.5),
        'ssm_C_re': nrm(ks[9], (DEPTH, 2, G, C, N), N ** -0.5),
        'ssm_C_im': nrm(ks[10], (DEPTH, 2, G, C, N), N ** -0.5),
        'ssm_D': nrm(ks[11], (DEPTH, S), 1.0),
        'ssm_w_glu': nrm(ks[12], (DEPTH, S, S), S ** -0.5),
        'w_ssm_out': nrm(ks[13], (DEPTH, S, D), S ** -0.5),
        'w_out': nrm(ks[14], (DEPTH, D, D), D ** -0.5),
        'ffn_norm_g': 1.0 + nrm(ks[15], (DEPTH, D), 0.02),
        'router_group_w': nrm(ks[16], (DEPTH, D, MOE_GROUPS), D ** -0.5),
        'router_group_b': nrm(ks[17], (DEPTH, MOE_GROUPS), 0.01),
        'router_expert_w': nrm(ks[18], (DEPTH, D, N_EXPERTS), D ** -0.5),
        'router_expert_b': nrm(ks[19], (DEPTH, N_EXPERTS), 0.01),
        'expert_w_gate': nrm(ks[20], (DEPTH, N_EXPERTS, D, D_EXPERT), D ** -0.5),
        'expert_w_up': nrm(ks[21], (DEPTH, N_EXPERTS, D, D_EXPERT), D ** -0.5),
        'expert_w_down': nrm(ks[22], (DEPTH, N_EXPERTS, D_EXPERT, D), D_EXPERT ** -0.5),
        'final_norm_g': 1.0 + nrm(ks[23], (D,), 0.02),
    }

def second_block(x, mix_norm_g, w_in, w_fourier_out, ssm_A_re, ssm_A_im, ssm_log_dt,
              ssm_B_re, ssm_B_im, ssm_C_re, ssm_C_im, ssm_D, ssm_w_glu, w_ssm_out,
              w_out, ffn_norm_g, router_group_w, router_group_b, router_expert_w,
              router_expert_b, expert_w_gate, expert_w_up, expert_w_down, final_norm_g):
    for i in range(DEPTH):
        h = _rmsnorm(x, mix_norm_g[i])
        z = h @ w_in[i]
        u_f = z[..., :FOURIER_WIDTH]
        u_s = z[..., FOURIER_WIDTH:FOURIER_WIDTH + SSM_WIDTH]
        gates = jax.nn.sigmoid(z[..., FOURIER_WIDTH + SSM_WIDTH:].astype(jnp.float32)).astype(x.dtype)
        y_f = _fourier_mix(u_f) @ w_fourier_out[i]
        y_s = _ssm_mix(u_s, ssm_A_re[i], ssm_A_im[i], ssm_log_dt[i], ssm_B_re[i], ssm_B_im[i],
                       ssm_C_re[i], ssm_C_im[i], ssm_D[i], ssm_w_glu[i]) @ w_ssm_out[i]
        merged = gates[..., :D_MODEL] * y_f + gates[..., D_MODEL:] * y_s
        x = x + merged @ w_out[i]
        hn = _rmsnorm(x, ffn_norm_g[i])
        x = x + _hier_moe(hn, router_group_w[i], router_group_b[i], router_expert_w[i],
                          router_expert_b[i], expert_w_gate[i], expert_w_up[i], expert_w_down[i])
    return _rmsnorm(x, final_norm_g)


def setup_inputs(seed=0):
    out = dict(first_inputs(seed))
    for name, value in second_inputs(seed + 1).items():
        if name != "x":
            out[name + "_2"] = value
    return out


def reference(
    x, norm1_w, w_in, cmp_pos_k, cmp_pos_v, cmp_k_w1, cmp_k_w2, cmp_v_w1, cmp_v_w2, conv_w,
    conv_b, lru_w_a, lru_b_a, lru_w_i, lru_b_i, lru_lambda, w_up_attn, w_up_rnn, w_out, norm2_w,
    mlp_w1, mlp_w2, final_norm_w, mix_norm_g_2, w_in_2, w_fourier_out_2, ssm_A_re_2, ssm_A_im_2,
    ssm_log_dt_2, ssm_B_re_2, ssm_B_im_2, ssm_C_re_2, ssm_C_im_2, ssm_D_2, ssm_w_glu_2,
    w_ssm_out_2, w_out_2, ffn_norm_g_2, router_group_w_2, router_group_b_2, router_expert_w_2,
    router_expert_b_2, expert_w_gate_2, expert_w_up_2, expert_w_down_2, final_norm_g_2,
):
    x = first_block(
        x, norm1_w, w_in, cmp_pos_k, cmp_pos_v, cmp_k_w1, cmp_k_w2, cmp_v_w1, cmp_v_w2, conv_w,
        conv_b, lru_w_a, lru_b_a, lru_w_i, lru_b_i, lru_lambda, w_up_attn, w_up_rnn, w_out,
        norm2_w, mlp_w1, mlp_w2, final_norm_w,
    )
    return second_block(
        x, mix_norm_g_2, w_in_2, w_fourier_out_2, ssm_A_re_2, ssm_A_im_2, ssm_log_dt_2,
        ssm_B_re_2, ssm_B_im_2, ssm_C_re_2, ssm_C_im_2, ssm_D_2, ssm_w_glu_2, w_ssm_out_2,
        w_out_2, ffn_norm_g_2, router_group_w_2, router_group_b_2, router_expert_w_2,
        router_expert_b_2, expert_w_gate_2, expert_w_up_2, expert_w_down_2, final_norm_g_2,
    )


_drawn_inputs = setup_inputs


def setup_inputs(seed=0):
    import zlib

    import numpy as np

    out = dict(_drawn_inputs(seed))
    spreads = {}
    factors = {'norm1_w': 3.29,
     'cmp_pos_k': 8.0,
     'lru_b_a': 8.0,
     'lru_b_i': 8.0,
     'mix_norm_g_2': 3.502,
     'ssm_A_re_2': 8.0,
     'ffn_norm_g_2': 3.037,
     'router_group_b_2': 4.107,
     'router_expert_b_2': 6.521,
     'final_norm_g_2': 2.838}
    for name, (base, spread) in spreads.items():
        noise = np.random.default_rng([zlib.crc32(name.encode()), seed]).standard_normal(out[name].shape)
        drawn = base * np.exp(spread * noise) if base else spread * noise
        out[name] = __import__('jax').numpy.asarray(drawn.astype(out[name].dtype))
    for name, factor in factors.items():
        out[name] = (out[name] * factor).astype(out[name].dtype)
    return out
```

```python
import functools
import math
from contextlib import ExitStack

import numpy as np
import concourse.bass as bass
from concourse import mybir

F32 = mybir.dt.float32
I32 = mybir.dt.int32
U32 = mybir.dt.uint32
ACT = mybir.ActivationFunctionType
ALU = mybir.AluOpType
AX = mybir.AxisListType

P = 128
CAP = 64

SM_COLS = {}


def _cols(table, spec):
    at = 0
    for name, n in spec:
        table[name] = (at, n)
        at += n
    return at


SM_N = _cols(SM_COLS, [("n1", 8), ("n2", 8), ("mix", 8), ("cw", 32), ("cb", 8), ("ba", 8), ("bi", 8),
                       ("lam", 8), ("dsk", 4), ("are", 32), ("aim", 32), ("ldt", 32), ("pk", 16), ("pv", 16),
                       ("kw2", 128), ("vw2", 128)])
CK_COLS = {}
CK_N = _cols(CK_COLS, [("ident", 128), ("neg", 128), ("cneg", 124), ("c01", 124), ("tri", 128), ("ones", 128),
                       ("iota", 128), ("tok", 4), ("cs", 256)])


class Buf:

    def __init__(self, ap, sem=None):
        self.ap = ap
        self.sem = sem
        self.free = []

    def take(self):
        assert self.free is not None, "taken while in use"
        w, self.free = self.free, None
        return w


class Ring:
    def __init__(self, bufs):
        self.bufs = bufs
        self.i = 0

    def take(self):
        b = self.bufs[self.i]
        self.i = (self.i + 1) % len(self.bufs)
        return b, b.take()


class Queue:

    def __init__(self, sems):
        self.q = {e: [] for e in "TVAGS"}
        self.sem = sems
        self.n = {}
        self.seen = {}

    def wait(self, e, toks):
        for t in toks:
            if t is None:
                continue
            if isinstance(t, list):
                self.wait(e, t)
                continue
            sem, v = t
            if self.seen.get((e, sem.name), 0) < v:
                self.seen[(e, sem.name)] = v
                self.q[e].append(lambda eng, s=sem, v=v: eng.wait_ge(s, v))

    def add(self, e, w, fn, sig=True):
        self.wait(e, w)
        if not sig:
            self.q[e].append(fn)
            return None
        s = self.sem[e]
        self.n[s.name] = self.n.get(s.name, 0) + 1
        self.q[e].append(lambda eng, f=fn, s=s: f(eng).then_inc(s, 1))
        return (s, self.n[s.name])

    def raw(self, e, fn):
        self.q[e].append(fn)

    def dma(self, e, w, out, in_, sem):
        self.wait(e, w)
        self.n[sem.name] = self.n.get(sem.name, 0) + 16
        self.q[e].append(lambda eng: eng.dma_start(out, in_).then_inc(sem, 16))
        return (sem, self.n[sem.name])

    def gather(self, w, out, in_, idx, sem):
        self.wait("G", w)
        self.n[sem.name] = self.n.get(sem.name, 0) + 16
        self.q["G"].append(lambda eng: eng.indirect_dma_start(
            out=out, out_offset=None, in_=in_,
            in_offset=bass.IndirectOffsetOnAxis(ap=idx, axis=0)).then_inc(sem, 16))
        return (sem, self.n[sem.name])

    def mm(self, w, out, lhsT, rhs, start, stop, sig=False):
        return self.add("T", w, lambda eng: eng.matmul(out, lhsT, rhs, start=start, stop=stop), sig)

    def tr(self, w, out, in_, ident, sig=False):
        return self.add("T", w, lambda eng: eng.transpose(out, in_, ident), sig)

    def act(self, w, out, in_, func, bias=0.0, scale=1.0, acc=None):
        if acc is None:
            return self.add("A", w, lambda eng: eng.activation(out, in_, func, bias=bias, scale=scale))
        return self.add("A", w, lambda eng: eng.activation(out, in_, func, bias=bias, scale=scale, accum_out=acc))

    def tt(self, e, w, out, a, b, op):
        return self.add(e, w, lambda eng: eng.tensor_tensor(out, a, b, op))

    def ts(self, e, w, out, a, s1, s2, op0, op1=None):
        if op1 is None:
            return self.add(e, w, lambda eng: eng.tensor_scalar(out, a, s1, None, op0))
        return self.add(e, w, lambda eng: eng.tensor_scalar(out, a, s1, s2, op0, op1))

    def stt(self, w, out, a, s, b, op0, op1):
        return self.add("V", w, lambda eng: eng.scalar_tensor_tensor(out, a, s, b, op0, op1))

    def cp(self, e, w, out, a):
        if e == "A":
            return self.act(w, out, a, ACT.Copy)
        return self.add(e, w, lambda eng: eng.tensor_copy(out, a))

    def red(self, w, out, a, op):
        return self.add("V", w, lambda eng: eng.tensor_reduce(out, a, op=op, axis=AX.X))

    def scan(self, w, out, a, b):
        return self.add("V", w, lambda eng: eng.tensor_tensor_scan(out, a, b, 0.0, ALU.mult, ALU.add))

    def rcp(self, w, out, a):
        return self.add("V", w, lambda eng: eng.reciprocal(out, a))

    def memset(self, e, w, out, v):
        return self.add(e, w, lambda eng: eng.memset(out, v))


def bc(ap, axis, n):
    a = ap.unsqueeze(axis)
    shape = list(a.shape)
    shape[axis] = n
    return a.to_broadcast(shape)


def weave(a, b, na, nb):
    live = [a, b]
    while any(live):
        for k, n in ((0, na), (1, nb)):
            for _ in range(n):
                if live[k] is not None and next(live[k], "end") == "end":
                    live[k] = None


def run(g):
    for _ in g:
        pass


def program(nc, A, out):
    ctx = ExitStack()
    with ctx:
        SB = ctx.enter_context(nc.sbuf_tensor("sb", [P, 53000], F32))
        PS = ctx.enter_context(nc.psum_tensor("ps", [P, 8 * 512], F32))
        names = {}

        def sem(n):
            names[n] = ctx.enter_context(nc.semaphore(n))
            return names[n]

        def dram(n, shape):
            return nc.dram_tensor(n, shape, F32).ap()

        hn_d = dram("hn_d", (512, 1024))
        y_d = dram("y_d", (4096, 1024))
        u_d = dram("u_d", (512, 512))
        yo_d = dram("yo_d", (512, 512))
        mbr_d = dram("mbr_d", (P, 32, 128))
        mbi_d = dram("mbi_d", (P, 32, 128))
        mcr_d = dram("mcr_d", (P, 32, 128))
        mci_d = dram("mci_d", (P, 32, 128))

        engine_sems = {e: sem("s" + e) for e in "TVAG"}
        Q = Queue(engine_sems)
        mm, tr, act, tt, ts, stt, cp, red, rcp = Q.mm, Q.tr, Q.act, Q.tt, Q.ts, Q.stt, Q.cp, Q.red, Q.rcp

        at = [0]

        def al(*shape):
            n = 1
            for d in shape:
                n *= d
            a = SB[:, at[0]:at[0] + n]
            at[0] += n
            assert at[0] <= 53000, at[0]
            if len(shape) == 2:
                a = a.rearrange("p (a b) -> p a b", b=shape[1])
            elif len(shape) == 3:
                a = a.rearrange("p (a b c) -> p a b c", b=shape[1], c=shape[2])
            return a

        def view(base, off, *shape):
            n = 1
            for d in shape:
                n *= d
            a = base[:, off:off + n]
            if len(shape) == 2:
                a = a.rearrange("p (a b) -> p a b", b=shape[1])
            elif len(shape) == 3:
                a = a.rearrange("p (a b c) -> p a b c", b=shape[1], c=shape[2])
            return a

        X = al(4, 1024)
        SMt = al(SM_N)
        CKt = al(CK_N)
        misc = al(400)
        RW = al(8 * 72)
        RB = al(72)
        H = al(8, 512)
        WR = [Buf(al(4096), sem(f"w{i}")) for i in range(4)]
        zone = al(53000 - at[0])
        ZN = zone.shape[1]
        zat = [0]

        def zal(*shape):
            n = 1
            for d in shape:
                n *= d
            a = view(zone, zat[0], *shape)
            zat[0] += n
            assert zat[0] <= ZN, (zat[0], ZN)
            return a

        banks = [Buf(PS[:, 512 * i:512 * i + 512]) for i in range(8)]

        def sm(n):
            a, k = SM_COLS[n]
            return SMt[:, a:a + k]

        def ck(n):
            a, k = CK_COLS[n]
            return CKt[:, a:a + k]

        mi = [0]

        def small(n):
            a = misc[:, mi[0]:mi[0] + n]
            mi[0] += n
            assert mi[0] <= 400
            return a

        ident = ck("ident")
        s_c = sem("s_c")
        s_x = sem("s_x")
        s_lru = sem("s_lru")
        t_x = Q.dma("S", [], X, A["x"].rearrange("(i p) d -> p i d", p=P), s_x)
        Q.dma("A", [], SMt, A["sm"], s_c)
        Q.dma("A", [], RW, A["rw"], s_c)
        Q.dma("A", [], RB, A["rb"].partition_broadcast(P), s_c)
        t_c = Q.dma("A", [], CKt, A["ck"], s_c)

        WQ = Ring(WR)

        def weights(src, n=4096):
            b, w = WQ.take()
            t = Q.dma("S", w, b.ap[:, 0:n], src, b.sem)
            return b, t

        def rstd_of(v, n, w, eps=1e-6):
            s = small(n)
            r = small(n)
            t = ts("V", w, v, v, 1.0 / 1024, eps, ALU.mult, ALU.add)
            ta = act([t], s, v, ACT.Sqrt)
            t = rcp([ta], r, s)
            t = tt("V", [t], s, r, r, ALU.mult)
            t = tt("V", [t], s, s, v, ALU.mult)
            t = ts("V", [t], s, s, -0.5, 1.5, ALU.mult, ALU.add)
            t = tt("V", [t], r, r, s, ALU.mult)
            return r, t

        def normed(xin, w, XN):
            v = small(4)
            t = None
            for i in range(4):
                t = act([w, t], XN[:, i, :], xin[:, i, :], ACT.Square, acc=v[:, i:i + 1])
            r, t = rstd_of(v, 4, [t])
            tk = None
            for i in range(4):
                tk = ts("V", [t], XN[:, i, :], xin[:, i, :], r[:, i:i + 1], None, ALU.mult)
            return tk

        def transposed(XN, w, HT, gain, pr, hw):
            toks = []
            for k in range(8):
                b, bw = pr.take()
                for i in range(4):
                    t = tr([w, bw], b.ap[:, 128 * i:128 * i + 128], XN[:, i, 128 * k:128 * k + 128], ident, sig=i == 3)
                g = gain[:, k:k + 1] if gain is not None else 1.0
                if k % 2:
                    t = act([t, t_c, hw], HT[:, k, :], b.ap, ACT.Copy, scale=g)
                else:
                    t = ts("V", [t, t_c, hw], HT[:, k, :], b.ap, g, None, ALU.mult)
                b.free = [t]
                toks.append(t)
            return toks

        def ftile(pr, wt, rhs, nk, w, last=True):
            b, bw = pr.take()
            t = None
            for k in range(nk):
                t = mm([w, bw], b.ap, wt(k), rhs(k), k == 0, k == nk - 1, sig=k == nk - 1)
            return b, t

        dense = Ring(banks[0:2])
        z0 = zat[0]
        XN = zal(4, 1024)
        T_ = view(zone, z0, 4, 512)
        GX = view(zone, z0 + 2048, 4, 512)
        GR = zal(8, 512)
        qT = zal(4, 512)
        kT = zal(2, 512)
        Vn = zal(4, 256)
        gate = zal(4, 24)
        z1 = zat[0]
        KC = [zal(2, 512), zal(2, 512)]
        BLK = [zal(16, 62), zal(16, 62)]
        PCT = view(zone, z1, 8, 512)
        zat[0] = max(zat[0], z1 + 4096)
        attnT = zal(4, 512)
        PR = [Buf(zal(2, 512)) for _ in range(2)]
        PTR = Ring([Buf(zal(512)) for _ in range(2)])
        XR = Ring([Buf(zal(515)) for _ in range(2)])
        XC = Ring([Buf(zal(512)) for _ in range(2)])
        TMP = Ring([Buf(zal(512)) for _ in range(3)])

        t_xn = normed(X, [t_x], XN)
        t_h = transposed(XN, [t_xn, t_c], H, sm("n1"), Ring(banks), [])
        xn_read = t_h

        def hk(k):
            return H[:, k, :]

        win = A["winF"]
        tiles = {}
        cur = {}

        def ftiles(src, total):
            state = {"g": -1}

            def get(m):
                g = m // 4
                if g != state["g"]:
                    n = min(4, total - 4 * g)
                    state["b"], state["t"] = weights(src[:, 4096 * g:4096 * g + 1024 * n], 1024 * n)
                    state["g"] = g
                b = state["b"]
                off = (m % 4) * 1024
                return b, state["t"], lambda k: b.ap[:, off + 128 * k:off + 128 * k + 128]
            return get

        getF = ftiles(win, 26)

        def proj(get, m, rhs, w, pr, total):
            b, t, wt = get(m)
            pb, tm = ftile(pr, wt, rhs, 8, [t, w])
            if m % 4 == 3 or m == total - 1:
                b.free = [tm]
            return pb, tm

        t_q = []
        for m in range(4):
            pb, t = proj(getF, m, hk, t_h, dense, 26)
            pb.free = [cp("AV"[m % 2], [t], qT[:, m, :], pb.ap)]
            t_q += pb.free
        t_k = []
        for m in range(2):
            pb, t = proj(getF, 4 + m, hk, t_h, dense, 26)
            pb.free = [cp("AV"[m % 2], [t], kT[:, m, :], pb.ap)]
            t_k += pb.free
        t_kc = [[], []]
        for m in range(4):
            pb, t = proj(getF, 6 + m, hk, t_h, dense, 26)
            dst = KC[m // 2][:, m % 2, :]
            ta = cp("A", [t], dst[0:64, :], pb.ap[0:64, :])
            tb = cp("V", [t], dst[64:128, 0:511], pb.ap[64:128, 1:512])
            pb.free = [ta, tb]
            t_kc[m // 2] += [ta, tb]

        bN, tN = weights(A["winN"], 8 * 280)
        wN = view(bN.ap, 0, 8, 280)
        t_v = []
        gz = []
        for i in range(4):
            b, bw = dense.take()
            for k in range(8):
                t = mm([t_h, tN, bw], b.ap[:, 0:280], H[:, k, 128 * i:128 * i + 128], wN[:, k, :], k == 0, k == 7, sig=k == 7)
            ta = cp("V", [t], Vn[:, i, :], b.ap[:, 0:256])
            tb = act([t, ta], gate[:, i, :], b.ap[:, 256:280], ACT.Tanh, scale=0.5)
            b.free = [ta, tb]
            t_v.append(ta)
            gz.append(tb)
        bN.free = [t]
        t_gate = ts("V", gz, gate, gate, 0.5, 0.5, ALU.mult, ALU.add)

        halfb = small(16)
        t_hb = ts("V", [t_c], halfb[:, 0:8], sm("ba"), 0.5, None, ALU.mult)
        t_hb = ts("V", [t_hb], halfb[:, 8:16], sm("bi"), 0.5, None, ALU.mult)

        def precise_exp(x, n, w):
            a, b = small(n), small(n)
            t = act(w, a, x, ACT.Tanh, scale=1.0 / 16)
            t = ts("V", [t], b, a, -1.0, 1.0, ALU.mult, ALU.add)
            t = rcp([t], b, b)
            t = stt([t], a, a, 1.0, b, ALU.add, ALU.mult)
            for _ in range(3):
                t = tt("V", [t], a, a, a, ALU.mult)
            return a, t

        sp = small(8)
        nab = small(8)
        t = ts("V", [t_c], nab, sm("lam"), -1.0, None, ALU.mult)
        t = tt("V", [t], nab, nab, sm("lam"), ALU.min)
        ew, t = precise_exp(nab, 8, [t])
        t = ts("V", [t], nab, ew, 2.0, None, ALU.add)
        t = rcp([t], nab, nab)
        t = tt("V", [t], ew, ew, nab, ALU.mult)
        z2 = small(8)
        t = tt("V", [t], z2, ew, ew, ALU.mult)
        t = ts("V", [t], nab, z2, 1.0 / 17, 1.0 / 15, ALU.mult, ALU.add)
        for d in (13, 11, 9, 7, 5, 3, 1):
            t = tt("V", [t], nab, nab, z2, ALU.mult)
            t = ts("V", [t], nab, nab, 1.0 / d, None, ALU.add)
        t = tt("V", [t], nab, nab, ew, ALU.mult)
        t = ts("V", [t], z2, sm("lam"), -1.0, 0.0, ALU.mult, ALU.max)
        t = stt([t], sp, nab, 2.0, z2, ALU.mult, ALU.add)
        m2sp = small(8)
        t_sp = ts("V", [t], m2sp, sp, -2.0, None, ALU.mult)

        lru = X.rearrange("p a b -> p (a b)")[:, 0:2048].rearrange("p (a b c) -> p a b c", a=2, b=8)
        tW = Q.dma("S", [t_xn], lru, A["lru"], s_lru)
        cw = sm("cw")

        def gelu2(src, w, dst):
            b1, w1 = TMP.take()
            t = act([w, w1], b1.ap, src, ACT.Square)
            t = ts("V", [t], b1.ap, b1.ap, 0.044715, 1.0, ALU.mult, ALU.add)
            t = tt("V", [t], b1.ap, b1.ap, src, ALU.mult)
            t = act([t], b1.ap, b1.ap, ACT.Tanh, scale=math.sqrt(2.0 / math.pi))
            t = stt([t], dst, b1.ap, 1.0, src, ALU.add, ALU.mult)
            b1.free = [t]
            return t

        t_gr = []
        t_rnn = []

        def recurrent():
            for half in range(2):
                t_T, t_G = [], []
                for q in range(4):
                    m = 4 * half + q
                    pb, t = proj(getF, 10 + 8 * half + q, hk, t_h, dense, 26)
                    xr, w = XR.take()
                    tz = Q.memset("G", w, xr.ap[:, 0:3], 0.0)
                    t = cp("A", [t, w], xr.ap[:, 3:515], pb.ap)
                    pb.free = [t]
                    xc, w = XC.take()
                    t = ts("V", [t, tz, w, t_c], xc.ap, xr.ap[:, 0:512], cw[:, m:m + 1], sm("cb")[:, m:m + 1], ALU.mult, ALU.add)
                    for j in range(1, 4):
                        t = stt([t], xc.ap, xr.ap[:, j:j + 512], cw[:, 8 * j + m:8 * j + m + 1], xc.ap, ALU.mult, ALU.add)
                    xr.free = [t]
                    tx = t
                    yield
                    for which in range(2):
                        b, bw = dense.take()
                        t = mm([tW, tx, bw], b.ap, lru[:, which, m, :], xc.ap, True, True, sig=True)
                        tmp, w = TMP.take()
                        ta = act([t, w, t_hb], tmp.ap, b.ap, ACT.Tanh, scale=0.5, bias=halfb[:, 8 * which + m:8 * which + m + 1])
                        b.free = [ta]
                        if which == 0:
                            t = act([ta, t_sp, xn_read, t_rnn[-1:]], T_[:, q, :], tmp.ap, ACT.Tanh,
                                    scale=m2sp[:, m:m + 1], bias=m2sp[:, m:m + 1])
                            t_T.append(t)
                        else:
                            t = stt([ta, t_rnn[-1:], xn_read], GX[:, q, :], tmp.ap, 1.0, xc.ap, ALU.add, ALU.mult)
                            xc.free = [t]
                            t_G.append(t)
                        tmp.free = [t]
                        yield
                for q in range(4):
                    m = 4 * half + q
                    pb, t = proj(getF, 14 + 8 * half + q, hk, t_h, dense, 26)
                    t = gelu2(pb.ap, [t], GR[:, m, :])
                    pb.free = [t]
                    t_gr.append(t)
                    yield
                for q in range(4):
                    m = 4 * half + q
                    Tm, Gm = T_[:, q, :], GX[:, q, :]
                    sq, w = TMP.take()
                    ta = act([t_T, w], sq.ap, Tm, ACT.Sqrt, scale=-1.0)
                    rc, w = TMP.take()
                    t = ts("V", [t_T, w], rc.ap, Tm, -1.0, 1.0, ALU.mult, ALU.add)
                    t = rcp([t], rc.ap, rc.ap)
                    t1 = stt([t, ta], Tm, Tm, 1.0, rc.ap, ALU.add, ALU.mult)
                    t = tt("V", [t1, ta], sq.ap, sq.ap, rc.ap, ALU.mult)
                    t = tt("V", [t, t_G], Gm, Gm, sq.ap, ALU.mult)
                    sq.free = [t]
                    t = Q.scan([t], rc.ap, Tm, Gm)
                    t = stt([t, t_gr], GR[:, m, :], rc.ap, 0.5, GR[:, m, :], ALU.mult, ALU.mult)
                    rc.free = [t]
                    t_rnn.append(t)
                    yield

        def compress():
            res = []
            for kv in range(2):
                b, tw = weights(A["cw1"][:, kv, :])
                w1 = view(b.ap, 0, 16, 256)
                pos = sm("pk" if kv == 0 else "pv")
                tb = []
                blk = BLK[kv].rearrange("p t (g n) -> p t g n", g=2)
                for g in range(2):
                    v = KC[kv][:, g, :].rearrange("p (n b two) -> p b n two", b=8, two=2)
                    for a in range(2):
                        tb.append(tt("V", [t_kc[kv], t_c], blk[:, 8 * a:8 * a + 8, g, :], v[:, :, a:a + 31, 0],
                                     bc(pos[:, 8 * a:8 * a + 8], 2, 31), ALU.add))
                hid, hw = TMP.take()
                hid4 = view(hid.ap, 0, 2, 62)
                th = []
                for ht in range(2):
                    pb, bw = dense.take()
                    for k in range(16):
                        t = mm([tw, tb, bw], pb.ap[:, 0:62], w1[:, k, 128 * ht:128 * ht + 128], BLK[kv][:, k, :], k == 0, k == 15, sig=k == 15)
                    src = pb.ap[:, 0:62]
                    u, uw = TMP.take()
                    ua = u.ap[:, 0:62]
                    t0 = t
                    t = act([t, uw], ua, src, ACT.Square)
                    t = ts("V", [t], ua, ua, 0.044715, 1.0, ALU.mult, ALU.add)
                    t = tt("V", [t], ua, ua, src, ALU.mult)
                    t = act([t], ua, ua, ACT.Tanh, scale=math.sqrt(2.0 / math.pi))
                    t = ts("V", [t], ua, ua, 1.0, 0.5, ALU.add, ALU.mult)
                    t = tt("V", [t, hw], hid4[:, ht, :], ua, src, ALU.mult)
                    u.free = [t]
                    pb.free = [t]
                    th.append(t)
                b.free = [t0]
                yield
                w2 = sm("kw2" if kv == 0 else "vw2").rearrange("p (a b) -> p a b", a=2)
                pb, bw = dense.take()
                if kv == 0:
                    for g in range(2):
                        for ht in range(2):
                            t = mm([th, bw, t_c], pb.ap[64 * g:64 * g + 64, 0:31], w2[:, ht, :], hid4[:, ht, 31 * g:31 * g + 31],
                                   ht == 0, ht == 1, sig=ht == 1)
                    kcT = small(31)
                    res.append(kcT)
                    tk = cp("V", [t], kcT, pb.ap[:, 0:31])
                else:
                    for g in range(2):
                        for ht in range(2):
                            t = mm([th, bw, t_c], pb.ap[0:31, 64 * g:64 * g + 64], hid4[:, ht, 31 * g:31 * g + 31], w2[:, ht, :],
                                   ht == 0, ht == 1, sig=ht == 1)
                    vc = small(128)
                    res.append(vc)
                    tk = cp("V", [t], vc[0:31, :], pb.ap[0:31, 0:128])
                pb.free = [tk]
                hid.free = [t]
                res.append(tk)
                yield
            cmpres.extend(res)

        cmpres = []
        t_attn = []
        attn_banks = banks[2:8]
        t_pct = []

        def cmp_scores():
            kcT, tkc, vc, tvc = cmpres
            for i in range(4):
                for h in range(2):
                    pb, bw = attn_banks[h], attn_banks[h].take()
                    ps3 = pb.ap[:, 0:124].rearrange("p (j n) -> p j n", j=4)
                    for j in range(4):
                        t = mm([tkc, t_q, bw], ps3[:, j, :], qT[64 * h:64 * h + 64, j, 128 * i:128 * i + 128],
                               kcT[64 * h:64 * h + 64, :], True, True, sig=j == 3)
                    sb, sw = TMP.take()
                    s3 = view(sb.ap, 0, 4, 31)
                    st = view(sb.ap, 124, 4, 1)[:, :, 0]
                    t = tt("V", [t, sw, t_c], s3, ps3, bc(ck("cneg")[:, 31 * i:31 * i + 31], 1, 4), ALU.add)
                    pb.free = [t]
                    t = red([t], st, s3, ALU.max)
                    t = tt("V", [t], s3, s3, bc(st, 2, 31), ALU.subtract)
                    t = act([t], s3, s3, ACT.Exp, scale=0.125)
                    t = tt("V", [t], s3, s3, bc(ck("c01")[:, 31 * i:31 * i + 31], 1, 4), ALU.mult)
                    t = red([t], st, s3, ALU.add)
                    t = ts("V", [t], st, st, 1e-20, None, ALU.max)
                    t = rcp([t], st, st)
                    gcol = gate[:, i, :].rearrange("p (hd c) -> p hd c", c=3)[:, 4 * h:4 * h + 4, 0]
                    t = tt("V", [t, t_gate], st, st, gcol, ALU.mult)
                    t = tt("V", [t], s3, s3, bc(st, 2, 31), ALU.mult)
                    p2, p2w = attn_banks[2 + h], attn_banks[2 + h].take()
                    for j in range(4):
                        t2 = tr([t, p2w], p2.ap[0:31, 128 * j:128 * j + 128], s3[:, j, :], ident, sig=j == 3)
                    sb.free = [t2]
                    t = cp("AV"[h], [t2, t_blk], PCT[0:31, 4 * h:4 * h + 4, 128 * i:128 * i + 128],
                           p2.ap[0:31, :].rearrange("p (a b) -> p a b", a=4))
                    p2.free = [t]
                    t_pct.append(t)
                    yield

        def attention():
            kcT, tkc, vc, tvc = cmpres
            SPs = [Buf(PS[:, 1024:2048].rearrange("p (a b) -> p a b", a=2)), Buf(PS[:, 2048:3072].rearrange("p (a b) -> p a b", a=2))]
            SPs[0].free = attn_banks[0].take() + attn_banks[1].take()
            SPs[1].free = attn_banks[2].take() + attn_banks[3].take()
            PTb, Ob = attn_banks[4], attn_banks[5]
            n = 0
            o_free = Ob.take()
            for j in range(4):
                o_toks = []
                for i in range(4):
                    nk = 128 * (i + 1)
                    for h in range(2):
                        hd = 4 * h + j
                        S = SPs[n % 2]
                        sw = S.take()
                        hs = slice(64 * h, 64 * h + 64)
                        for ty in range(2):
                            mm([t_q, t_k, sw], S.ap[:, ty, 0:nk], qT[hs, j, 128 * i:128 * i + 128], kT[hs, ty, 0:nk], True, False)
                            t = mm([t_c], S.ap[:, ty, nk - 128:nk], ident, ck("neg"), False, True, sig=True)
                        st = ST[n % 2]
                        mx, rs = st.ap[:, 0:2], st.ap[:, 2:4]
                        pr = PR[n % 2]
                        pw = pr.take()
                        t = red([t, st.take()], mx, S.ap[:, :, 0:nk], ALU.max)
                        t = ts("V", [t], mx, mx, -0.125, None, ALU.mult)
                        te = None
                        for ty in range(2):
                            te = act([t, pw], pr.ap[:, ty, 0:nk], S.ap[:, ty, 0:nk], ACT.Exp, bias=mx[:, ty:ty + 1], scale=0.125,
                                     acc=rs[:, ty:ty + 1])
                        S.free = [te]
                        t = ts("V", [te], rs, rs, 1e-20, None, ALU.max)
                        t = rcp([t], rs, rs)
                        t = tt("V", [t, t_gate], rs, rs, gate[:, i, 3 * hd + 1:3 * hd + 3], ALU.mult)
                        dg = DG[n % 2]
                        dw = dg.take()
                        for ty in range(2):
                            td = ts("V", [t, dw], dg.ap[:, ty, :], ident, rs[:, ty:ty + 1], None, ALU.mult)
                        st.free = [td]
                        yield
                        for ty in range(2):
                            ptw = PTb.take()
                            for kb in range(i + 1):
                                t = mm([te, td, ptw], PTb.ap[:, 128 * kb:128 * kb + 128], pr.ap[:, ty, 128 * kb:128 * kb + 128],
                                       dg.ap[:, ty, :], True, True, sig=kb == i)
                            pt, ptsw = PTR.take()
                            tp = cp("AV"[ty], [t, ptsw], pt.ap[:, 0:nk], PTb.ap[:, 0:nk])
                            PTb.free = [tp]
                            if ty == 1:
                                pr.free = [t]
                                dg.free = [t]
                            yield
                            for kb in range(i + 1):
                                t = mm([tp, t_v, o_free], Ob.ap[hs, 128 * i:128 * i + 128],
                                       Vn[:, kb, 128 * ty + 64 * h:128 * ty + 64 * h + 64], pt.ap[:, 128 * kb:128 * kb + 128],
                                       ty == 0 and kb == 0, False, sig=kb == i)
                            pt.free = [t]
                        t = mm([tvc, t_pct], Ob.ap[hs, 128 * i:128 * i + 128], vc[0:31, 64 * h:64 * h + 64], PCT[0:31, hd, 128 * i:128 * i + 128],
                               False, True, sig=True)
                        o_toks.append(t)
                        n += 1
                        yield
                t = cp("V", [o_toks], attnT[:, j, :], Ob.ap)
                o_free = [t]
                t_attn.append(t)
            Ob.free = o_free
            attn_banks[0].free = attn_banks[1].free = SPs[0].free
            attn_banks[2].free = attn_banks[3].free = SPs[1].free

        ST = [Buf(small(4)) for _ in range(2)]
        DG = [Buf(zal(2, 128)) for _ in range(2)]

        run(compress())
        t_blk = [cmpres[1], cmpres[3]]
        run(cmp_scores())
        weave(attention(), recurrent(), 2, 1)

        allb = Ring(banks)
        t_x = Q.dma("S", [t_rnn], X, A["x"].rearrange("(i p) d -> p i d", p=P), s_x)
        MG = XN

        def merge(src, m, pieces, w, dst, pr, tmp, size=3584):
            b, tw = weights(src[:, size * m:size * m + size], size)
            pbs = []
            for off, rhs, nk in pieces:
                pbs.append(ftile(pr, lambda k, off=off: b.ap[:, off + 128 * k:off + 128 * k + 128], rhs, nk, [tw, w]))
            b.free = [pbs[-1][1]]
            out_t = []
            half = []
            for g in range(2):
                x, xw = tmp.take()
                pg, tg = pbs[g]
                py, ty = pbs[2 + g]
                t = act([tg, xw], x.ap, pg.ap, ACT.Tanh, scale=0.5)
                pg.free = [t]
                t = stt([t, ty], x.ap, x.ap, 1.0, py.ap, ALU.add, ALU.mult)
                py.free = [t]
                half.append((x, t))
            t = tt("V", [half[0][1], half[1][1], w], dst, half[0][0].ap, half[1][0].ap, ALU.add)
            half[0][0].free = [t]
            half[1][0].free = [t]
            return t

        t_mg = []
        for m in range(8):
            t_mg.append(merge(A["mg1"], m, [(0, hk, 8), (1024, hk, 8), (2048, lambda k: attnT[:, k, :], 4),
                                            (2560, lambda k: GR[:, k, :], 8)], [t_h, t_attn, t_rnn], MG[:, m // 2, 512 * (m % 2):512 * (m % 2) + 512],
                              allb, TMP))

        def residual(src, MGk, w):
            t_r = []
            tl = None
            for nh in range(2):
                b, tw = weights(src[:, 4096 * nh:4096 * nh + 4096])
                w_ = view(b.ap, 0, 8, 512)
                for i in range(4):
                    pb, bw = allb.take()
                    for k in range(8):
                        t = mm([tw, w, bw], pb.ap, MGk(k)[:, 128 * i:128 * i + 128], w_[:, k, :], k == 0, k == 7, sig=k == 7)
                    tl = t
                    xs = X[:, i, 512 * nh:512 * nh + 512]
                    t = stt([t, t_x], xs, pb.ap, 0.5, xs, ALU.mult, ALU.add)
                    pb.free = [t]
                    t_r.append(t)
                b.free = [tl]
            return t_r, tl

        t_x1, t_last = residual(A["wo1"], lambda k: MG[:, k // 2, 512 * (k % 2):512 * (k % 2) + 512], t_mg)

        t_xn = normed(X, [t_x1, t_last], XN)
        t_h = transposed(XN, [t_xn], H, sm("n2"), allb, [t_last])
        HT = view(zone, 4096, 32, 512)
        b0, b1_ = 0, 20480
        PB = view(zone, b0, 2, 32, 8)
        PC = view(zone, b0 + 512, 2, 32, 8)
        BB = view(zone, b0 + 1024, 2, 32, 16)
        CC = view(zone, b0 + 2048, 2, 32, 16)
        sat = [b0 + 3072]

        def s32(*shape):
            n = 1
            for d in shape:
                n *= d
            a = view(zone, sat[0], *shape)
            sat[0] += n
            assert sat[0] <= b0 + 4096
            return a

        nC = s32(512)
        BZ = view(zone, b1_, 4, 512)
        T1 = view(zone, b1_ + 2048, 512)
        T2 = view(zone, b1_ + 2560, 512)
        Mr = view(zone, b1_ + 3072, 512)
        Mi = view(zone, b1_ + 3584, 512)
        Zt = view(zone, b1_ + 4096, 1088)
        keep = ck("neg")
        U8 = keep[:, 0:64].rearrange("p (a b) -> p a b", a=2)
        RHO8 = keep[:, 64:96]
        cm_tmp = ck("cneg")[:, 0:124]
        s_bc = sem("s_bc")

        def cmul(out, x, y, _, w):
            a = cm_tmp[:, 0:64].rearrange("p (a b) -> p a b", a=2)
            b = ck("c01")[:, 0:64].rearrange("p (a b) -> p a b", a=2)
            t1 = tt("V", w, a, x, bc(y[:, 0, :], 1, 2), ALU.mult)
            t2 = tt("V", w, b, x, bc(y[:, 1, :], 1, 2), ALU.mult)
            t = tt("V", [t1, t2], out[:, 0, :], a[:, 0, :], b[:, 1, :], ALU.subtract)
            return tt("V", [t], out[:, 1, :], a[:, 1, :], b[:, 0, :], ALU.add)

        def wide_exp(x, w):
            a, b = s32(32), s32(32)
            t = act(w, a, x, ACT.Tanh, scale=1.0 / 16)
            t = ts("V", [t], b, a, -1.0, 1.0, ALU.mult, ALU.add)
            t = rcp([t], b, b)
            t = stt([t], a, a, 1.0, b, ALU.add, ALU.mult)
            for _ in range(3):
                t = tt("V", [t], a, a, a, ALU.mult)
            return a, t

        t_store = []
        ssm_state = {}

        def ssm_prep(w0, pr):
            w0 = [w0, t_c]
            t_bb = Q.dma("A", w0, BB.rearrange("p a b c -> p (a b c)"), A["bb"], s_bc)
            t_bb = Q.dma("A", w0, CC.rearrange("p a b c -> p (a b c)"), A["cc"], s_bc)
            dt, t = wide_exp(sm("ldt"), w0)
            x = s32(32)
            t = tt("V", [t], x, sm("are"), dt, ALU.mult)
            th = dt
            t = tt("V", [t], th, sm("aim"), dt, ALU.mult)
            ea, t = wide_exp(x, [t])
            k = x
            t = ts("V", [t], k, th, 1.0 / (2 * math.pi), 12582912.0, ALU.mult, ALU.add)
            t = ts("V", [t], k, k, 12582912.0, None, ALU.subtract)
            t = stt([t], th, k, -6.28125, th, ALU.mult, ALU.add)
            t = stt([t], th, k, -(2 * math.pi - 6.28125), th, ALU.mult, ALU.add)
            t = ts("V", [t], th, th, 3.1415925, -3.1415925, ALU.min, ALU.max)
            yield
            u = s32(2, 32)
            a1 = s32(2, 32)
            ta = act([t], u[:, 1, :], th, ACT.Sin)
            ta = act([t], u[:, 0, :], th, ACT.Sin, scale=0.5)
            t = tt("V", [ta], u[:, 0, :], u[:, 0, :], u[:, 0, :], ALU.mult)
            t = ts("V", [t], u[:, 0, :], u[:, 0, :], -2.0, 1.0, ALU.mult, ALU.add)
            t = tt("V", [t], a1, u, bc(ea, 1, 2), ALU.mult)
            t_a = t
            t = tt("V", [t], ea, ea, ea, ALU.mult)
            t = tt("V", [t], ea, ea, ea, ALU.mult)
            t = tt("V", [t], RHO8, ea, ea, ALU.mult)
            t = cmul(U8, u, u, None, [t])
            t = cmul(u, U8, U8, None, [t])
            t = cmul(U8, u, u, None, [t])
            ssm_state["t"] = t
            yield
            cur = [s32(2, 32), s32(2, 32)]
            g = Q.memset("V", [t], cur[0][:, 0, :], 1.0)
            t = Q.memset("V", [g], cur[0][:, 1, :], 0.0)
            tg = None
            rel = [None, None]
            for j in range(9):
                c = cur[j % 2]
                lo, hi = slice(0, 64), slice(64, 128)
                if j < 8:
                    tg = cp("G", [t, tg], PB[lo, :, :, 7 - j], c[lo])
                    tg = cp("G", [t, tg], PB[hi, :, :, j], c[hi])
                if j > 0:
                    tg = cp("G", [t, tg], PC[lo, :, :, j - 1], c[lo])
                    tg = cp("G", [t, tg], PC[hi, :, :, 8 - j], c[hi])
                rel[j % 2] = tg
                if j < 8:
                    t = cmul(cur[1 - j % 2], c, a1, None, [t, rel[1 - j % 2], t_a])
                if j % 3 == 2:
                    yield
            t_pw = tg
            lr, li = sm("are"), sm("aim")
            am = cur[1]
            t = ts("V", [t, t_pw], am[:, 0, :], a1[:, 0, :], -1.0, None, ALU.add)
            f = u
            q_, r_ = th, ea
            t = tt("V", [t], q_, lr, lr, ALU.mult)
            t = tt("V", [t], r_, li, li, ALU.mult)
            t = tt("V", [t], q_, q_, r_, ALU.add)
            t = rcp([t], q_, q_)
            t = tt("V", [t], f[:, 0, :], am[:, 0, :], lr, ALU.mult)
            t = tt("V", [t], r_, a1[:, 1, :], li, ALU.mult)
            t = tt("V", [t], f[:, 0, :], f[:, 0, :], r_, ALU.add)
            t = tt("V", [t], f[:, 1, :], a1[:, 1, :], lr, ALU.mult)
            t = tt("V", [t], r_, am[:, 0, :], li, ALU.mult)
            t = tt("V", [t], f[:, 1, :], f[:, 1, :], r_, ALU.subtract)
            t = tt("V", [t], f, f, bc(q_, 1, 2), ALU.mult)
            yield
            v = lambda a: a.rearrange("p (a b) -> p a b", a=32)
            fr, fi = bc(f[:, 0, :], 2, 16), bc(f[:, 1, :], 2, 16)
            w = [t, t_bb]
            t1 = tt("V", w, v(T1), BB[:, 0], fr, ALU.mult)
            t2 = tt("V", w, v(T2), BB[:, 1], fi, ALU.mult)
            t3 = tt("V", w, v(Mr), BB[:, 0], fi, ALU.mult)
            t4 = tt("V", w, v(Mi), BB[:, 1], fr, ALU.mult)
            t = tt("V", [t1, t2, t3, t4], BB[:, 0], v(T1), v(T2), ALU.subtract)
            t = tt("V", [t], BB[:, 1], v(Mr), v(Mi), ALU.add)
            tz = Q.memset("G", [w0, tg], BZ, 0.0)
            flat = BB.rearrange("p a b c -> p a (b c)")
            t_bz = []
            for ri in range(2):
                t_bz.append(cp("V", [t, tz], BZ[0:64, ri, :], flat[0:64, ri, :]))
                t_bz.append(cp("V", [t, tz], BZ[64:128, 2 + ri, :], flat[64:128, ri, :]))
            t_nc = ts("V", [t_bb, t_bz[-1]], nC, CC[:, 1].rearrange("p a b -> p (a b)"), -1.0, None, ALU.mult)
            t_pw = [t_pw, t_nc]
            yield
            s_st = sem("s_st")
            m_free, T_free, Z_free = [t_nc], [t_nc], []
            c4 = lambda a: a.rearrange("p (a b c) -> p a b c", a=4, b=8)
            zd = A["z_d"]
            for c in range(8):
                gs = slice(4 * c, 4 * c + 4)

                def outer(pwt, mat, oo, kind, w):
                    p0, p1 = bc(pwt[:, 0, gs, :], 3, 16), bc(pwt[:, 1, gs, :], 3, 16)
                    m0, m1 = bc(mat[:, 0, gs, :], 2, 8), bc(mat[:, 1, gs, :], 2, 8)
                    t1 = tt("V", w, c4(T1), p0, m0, ALU.mult)
                    t2 = tt("G", w, c4(T2), p1, m1, ALU.mult)
                    ta = tt("V", [t1, t2, w], Mr, T1, T2, ALU.subtract)
                    t1 = tt("V", [ta], c4(T1), p0, m1, ALU.mult)
                    t2 = tt("G", [ta], c4(T2), p1, m0, ALU.mult)
                    if kind:
                        t1 = tt("V", [t1, t2], Mi, T1, T2, ALU.add)
                        return ts("V", [t1], Mi, Mi, -1.0, None, ALU.mult)
                    return tt("V", [t1, t2], Mi, T1, T2, ALU.add)

                t = outer(PB, BB, 0, False, [m_free, T_free, t_pw])
                pb, bw = pr.take()
                pb2_, bw2 = pr.take()
                for q in range(4):
                    tr([t, bw, t_c], pb.ap[:, 128 * q:128 * q + 128], Mr[:, 128 * q:128 * q + 128], ident)
                for q in range(4):
                    tp = tr([t, bw2], pb2_.ap[:, 128 * q:128 * q + 128], Mi[:, 128 * q:128 * q + 128], ident, sig=q == 3)
                t1 = cp("A", [tp], T1, pb.ap)
                t2 = cp("A", [tp], T2, pb2_.ap)
                pb.free = [t1]
                pb2_.free = [t2]
                d1 = Q.dma("A", [t1], mbr_d[:, gs, :], T1.rearrange("p (a b) -> p a b", a=4), s_st)
                d1 = Q.dma("A", [t2], mbi_d[:, gs, :], T2.rearrange("p (a b) -> p a b", a=4), s_st)
                T_free = [d1]
                m_free = [tp]
                yield
                t = outer(PC, CC, 0, True, [m_free, T_free, t_pw])
                d2 = Q.dma("A", [t], mcr_d[:, gs, :], Mr.rearrange("p (a b) -> p a b", a=4), s_st)
                d2 = Q.dma("A", [t], mci_d[:, gs, :], Mi.rearrange("p (a b) -> p a b", a=4), s_st)
                T_free = [t]
                zt = []
                for q in range(4):
                    gg = 4 * c + q
                    pb, bw = pr.take()
                    cols = slice(16 * gg, 16 * gg + 16)
                    for at0, n, zr, ri_, rhs in (
                            (0, 128, BZ[:, 2, cols], BZ[:, 3, cols], (Mr[:, 128 * q:128 * q + 128], Mi[:, 128 * q:128 * q + 128])),
                            (128, 16, flat[:, 0, cols], flat[:, 1, cols], (CC[:, 0, gg, :], nC[:, cols])),
                            (144, 128, BZ[:, 0, cols], BZ[:, 1, cols], (Mr[:, 128 * q:128 * q + 128], Mi[:, 128 * q:128 * q + 128]))):
                        mm([t, bw, t_nc], pb.ap[0:16, at0:at0 + n], zr, rhs[0], True, False)
                        tp = mm([], pb.ap[0:16, at0:at0 + n], ri_, rhs[1], False, True, sig=at0 == 144)
                    t1 = cp("A", [tp, Z_free], Zt[0:16, 272 * q:272 * q + 272], pb.ap[0:16, 0:272])
                    pb.free = [t1]
                    zt.append(t1)
                d3 = Q.dma("A", zt, zd[:, gs, :], Zt[0:16, :].rearrange("p (a b) -> p a b", a=4), s_st)
                Z_free = [d3]
                m_free = [tp, d2, d3]
                yield
            t_store.append(d3)

        mcr_load = None

        def weights_from(src, w):
            b, w2 = WQ.take()
            if isinstance(src, str):
                for ji in range(8):
                    t = Q.dma("S", [w, w2], b.ap[16 * ji:16 * ji + 16, :].rearrange("p (a b) -> p a b", a=32),
                              A["z_d"][:, :, 16 * (8 - ji):16 * (8 - ji) + 128], b.sem)
                return b, t
            t = Q.dma("S", [w, w2], b.ap, src.rearrange("p a b -> p (a b)"), b.sem)
            return b, t

        dd_load = "z"
        A["z_d"] = dram("z_d", (16, 32, 272))
        run(ssm_prep([t_h], allb))
        t_ssm = ssm_state["t"]
        getM = ftiles(A["m1"], 32)
        t_m = []
        for m in range(32):
            pb, t = proj(getM, m, hk, t_h, allb, 32)
            t = act([t], HT[:, m, :], pb.ap, ACT.Relu)
            pb.free = [t]
            t_m.append(tt("V", [t], HT[:, m, :], HT[:, m, :], HT[:, m, :], ALU.mult))
        bw = [b.take() for b in banks]
        for s_ in range(8):
            b, tw = weights(A["m2"][:, 4096 * s_:4096 * s_ + 4096])
            w_ = view(b.ap, 0, 4, 1024)
            for q in range(4):
                k = 4 * s_ + q
                for i in range(4):
                    for nh in range(2):
                        t = mm([tw, t_m[k], bw[2 * i + nh]], banks[2 * i + nh].ap, HT[:, k, 128 * i:128 * i + 128],
                               w_[:, q, 512 * nh:512 * nh + 512], k == 0, k == 31, sig=(k == 31 or (q == 3 and i == 3 and nh == 1)))
                        if k == 31:
                            xs = X[:, i, 512 * nh:512 * nh + 512]
                            banks[2 * i + nh].free = [tt("V", [t], xs, xs, banks[2 * i + nh].ap, ALU.add)]
            b.free = [t]
        t_x2 = [b.free[0] for b in banks]

        row = view(zone, 24576, 1024)

        def rowload(name, w, s):
            return Q.dma("A", w, row, A[name].partition_broadcast(P), s)

        s_row = sem("s_row")
        zfree = [t_x2, t_store]
        t_row = rowload("fn1", zfree, s_row)
        t_xn = normed(X, [t_x2], XN)
        t = None
        t_xb = []
        for i in range(4):
            t_xb.append(tt("V", [t_xn, t_row], X[:, i, :], XN[:, i, :], row, ALU.mult))
        t_x = t_xb
        t_xn = normed(X, [t_xb], XN)
        t_h = transposed(XN, [t_xn], H, sm("mix"), allb, [])

        Vp = view(zone, 0, 2, 32, 64)
        Vf = view(zone, 4096, 4, 4, 256)
        tmpA = view(zone, 4096, 2, 32, 64)
        ufT = view(zone, 8192, 4, 512)
        RHO = view(zone, 8192, 32, 64)
        usT = view(zone, 10240, 4, 512)
        yfT = view(zone, 12288, 4, 512)
        U = view(zone, 14336, 32, 64)
        Ep = view(zone, 16384, 2, 32, 64)
        Sp = view(zone, 20480, 2, 32, 64)

        getZ = ftiles(A["z2"], 8)
        t_uf, t_us = [], []
        for m in range(4):
            pb, t = proj(getZ, m, hk, t_h, allb, 8)
            pb.free = [cp("AV"[m % 2], [t, t_xb], ufT[:, m, :], pb.ap)]
            t_uf += pb.free
        for m in range(4):
            pb, t = proj(getZ, 4 + m, hk, t_h, allb, 8)
            dst = usT[:, m, :].rearrange("p (j k) -> p j k", j=8)
            pb.free = [cp("AV"[m % 2], [t], dst, pb.ap.rearrange("p (k j) -> p j k", j=8))]
            t_us += pb.free
        s_u = sem("s_u")
        t_ud = Q.dma("A", [t_us], u_d.rearrange("(m p) t -> p m t", p=P), usT, s_u)
        s_u2 = sem("s_u2")
        uv = u_d.rearrange("(g c) (j k) -> j c g k", c=16, j=8)
        for j in range(8):
            t_U = Q.dma("A", [t_ud], U[16 * j:16 * j + 16, :, :], uv[j], s_u2)

        bF, tF = weights(A["dft"])
        cf = view(bF.ap, 0, 2, 4, 512)
        t_vf = []
        for i in range(4):
            for gp in range(2):
                pb, bw = allb.take()
                for q in range(2):
                    t = mm([t_uf, bw, t_c], pb.ap[:, 256 * q:256 * q + 256], ufT[:, 2 * gp + q, 128 * i:128 * i + 128], ck("cs"),
                           True, True, sig=q == 1)
                pb.free = [cp("AV"[gp], [t], Vf[:, i, 2 * gp:2 * gp + 2, :], pb.ap.rearrange("p (a b) -> p a b", a=2))]
                t_vf += pb.free
        t_yf = []
        for g in range(4):
            pb, bw = allb.take()
            for k in range(8):
                t = mm([t_vf, tF, bw], pb.ap, Vf[:, k % 4, g, 128 * (k // 4):128 * (k // 4) + 128], cf[:, k // 4, k % 4, :], k == 0, k == 7, sig=k == 7)
            pb.free = [cp("AV"[g % 2], [t], yfT[:, g, :], pb.ap)]
            t_yf += pb.free
        bF.free = [t]
        t_f_last = t

        te = Q.memset("G", [t_h], Ep[:, 0, :, 0], 1.0)
        te = Q.memset("G", [t_h], Ep[:, 1, :, 0], 0.0)
        pw = U8
        tpw = t_ssm
        pb2 = [view(zone, 4096 + 2048 + 64 * q, 2, 32) for q in range(2)]
        big = view(zone, 4096, 2048)
        for q in range(6):
            n = 1 << q
            ta = bc(pw[:, 0, :], 2, n)
            tb = bc(pw[:, 1, :], 2, n)
            er, ei = Ep[:, 0, :, 0:n], Ep[:, 1, :, 0:n]
            o_r, o_i = Ep[:, 0, :, n:2 * n], Ep[:, 1, :, n:2 * n]
            tm = view(big, 0, 32, 64)[:, :, 0:n]
            w = [te, tpw, t_f_last]
            t = tt("V", w, o_r, er, ta, ALU.mult)
            t1 = tt("V", w, tm, ei, tb, ALU.mult)
            t = tt("V", [t, t1], o_r, o_r, tm, ALU.subtract)
            t2 = tt("V", [t], o_i, er, tb, ALU.mult)
            t1 = tt("V", [t], tm, ei, ta, ALU.mult)
            te = tt("V", [t1, t2], o_i, o_i, tm, ALU.add)
            if q < 5:
                nx = pb2[q % 2]
                tpw = cmul(nx, pw, pw, view(big, 2048 - 128, 2, 32) if False else cm_tmp, [tpw, te])
                pw = nx
        t_E = te
        t_rho = cp("V", [t_vf, t_f_last, t_ssm, t_yf], RHO, bc(RHO8, 2, 64))
        t_rho = Q.memset("V", [t_rho], RHO[:, :, 0], 0.0)

        t_V = []
        for ri, src in ((0, mbr_d), (1, mbi_d)):
            b, tw = weights_from(src, t_store)
            w_ = view(b.ap, 0, 32, 128)
            for g8 in range(4):
                pb, bw = allb.take()
                for q in range(8):
                    g = 8 * g8 + q
                    t = mm([tw, t_U, bw], pb.ap[:, 64 * q:64 * q + 64], w_[:, g, :], U[:, g, :], True, True, sig=q == 7)
                src3 = pb.ap.rearrange("p (a b) -> p a b", a=8)
                dst = Vp[:, ri, 8 * g8:8 * g8 + 8, :]
                ta = cp("A", [t], dst[0:64], src3[0:64])
                tb = cp("V", [t], dst[64:128], src3[64:128, :, ::-1])
                pb.free = [ta, tb]
                t_V += [ta, tb]
            b.free = [t]
        vr, vi, er, ei = Vp[:, 0], Vp[:, 1], Ep[:, 0], Ep[:, 1]
        ar, ai = tmpA[:, 0], tmpA[:, 1]
        w = [t_V, t_E, t_rho]
        gr_, gi_ = Sp[:, 0], Sp[:, 1]
        t1 = tt("V", w, ar, vr, er, ALU.mult)
        t2 = tt("V", w, ai, vi, ei, ALU.mult)
        t3 = tt("V", w, gr_, vi, er, ALU.mult)
        t4 = tt("V", w, gi_, vr, ei, ALU.mult)
        t5 = tt("V", [t1, t2, t4], vr, ar, ai, ALU.add)
        t6 = tt("V", [t3, t4, t5], vi, gr_, gi_, ALU.subtract)

        def fl(a):
            return a.rearrange("p a b -> p (a b)")
        t7 = Q.scan([t5, t6], fl(ar), fl(RHO), fl(vr))
        t8 = Q.scan([t6, t7], fl(ai), fl(RHO), fl(vi))
        t1 = tt("V", [t7], vr, ar, er, ALU.mult)
        t2 = tt("V", [t8], vi, ai, ei, ALU.mult)
        tz = Q.memset("G", [t6], Sp[0:64, :, :, 0], 0.0)
        tz = Q.memset("G", [t6, tz], Sp[64:128, :, :, 63], 0.0)
        t_S = []
        f_, b_ = slice(0, 64), slice(64, 128)
        t_S.append(tt("V", [t1, t2, tz, t6], gr_[f_, :, 1:64], vr[f_, :, 0:63], vi[f_, :, 0:63], ALU.subtract))
        t_S.append(tt("V", [t1, t2, tz], gr_[b_, :, 62::-1], vr[b_, :, 0:63], vi[b_, :, 0:63], ALU.subtract))
        t1 = tt("V", [t_S], vr, ar, ei, ALU.mult)
        t2 = tt("V", [t_S], vi, ai, er, ALU.mult)
        t_S.append(tt("V", [t1, t2, tz], gi_[f_, :, 1:64], vr[f_, :, 0:63], vi[f_, :, 0:63], ALU.add))
        t_S.append(tt("V", [t1, t2, tz], gi_[b_, :, 62::-1], vr[b_, :, 0:63], vi[b_, :, 0:63], ALU.add))

        slots = []
        for src in (dd_load, mcr_d, mci_d):
            slots.append(weights_from(src, t_store))
        YS = view(zone, 4096, 32, 64)
        t_y = []
        for g8 in range(4):
            pb, bw = allb.take()
            for q in range(8):
                g = 8 * g8 + q
                for k, rhs in enumerate((U[:, g, :], Sp[:, 0, g, :], Sp[:, 1, g, :])):
                    b, tw = slots[k]
                    t = mm([tw, t_S, bw, t_U], pb.ap[:, 64 * q:64 * q + 64], b.ap[:, 128 * g:128 * g + 128], rhs, k == 0, k == 2, sig=k == 2 and q == 7)
            pb.free = [cp("AV"[g8 % 2], [t, t_S], YS[:, 8 * g8:8 * g8 + 8, :], pb.ap.rearrange("p (a b) -> p a b", a=8))]
            t_y += pb.free
        for b, _ in slots:
            b.free = [t]
        s_y1 = sem("s_y1")
        s_y2 = sem("s_y2")
        yv = yo_d.rearrange("(g c) (j k) -> j c g k", c=16, j=8)
        for j in range(8):
            t_yd = Q.dma("A", [t_y], yv[j], YS[16 * j:16 * j + 16, :, :], s_y1)
        yT = view(zone, 0, 4, 512)
        yG = view(zone, 2048, 4, 512)
        t_yl = Q.dma("A", [t_yd, t_S], yT, yo_d.rearrange("(m p) t -> p m t", p=P), s_y2)
        TM2 = Ring([Buf(view(zone, 6144 + 512 * q, 512)) for q in range(4)])
        t_g = []
        for m in range(4):
            b1, w1 = TM2.take()
            y = yT[:, m, :]
            t = stt([t_yl, t_c, t_y], y, usT[:, m, :], sm("dsk")[:, m:m + 1], y, ALU.mult, ALU.add)
            t = act([t, w1], b1.ap, y, ACT.Square)
            t = ts("V", [t], b1.ap, b1.ap, 0.044715, 1.0, ALU.mult, ALU.add)
            t = tt("V", [t], b1.ap, b1.ap, y, ALU.mult)
            t = act([t], b1.ap, b1.ap, ACT.Tanh, scale=math.sqrt(2.0 / math.pi))
            t = ts("V", [t], b1.ap, b1.ap, 1.0, 0.5, ALU.add, ALU.mult)
            t = tt("V", [t], y, b1.ap, y, ALU.mult)
            b1.free = [t]
            t_g.append(t)
        bG, tG = weights(A["glu"], 2048)
        wg_ = view(bG.ap, 0, 4, 4, 128)
        t_ys = []
        for m in range(4):
            pb, t = ftile(allb, lambda k: wg_[:, m, k, :], lambda k: yT[:, k, :], 4, [tG, t_g])
            b1, w1 = TM2.take()
            t_gl = t
            t = act([t, w1], b1.ap, pb.ap, ACT.Tanh, scale=0.5)
            pb.free = [t]
            t = ts("V", [t], b1.ap, b1.ap, 1.0, 0.5, ALU.add, ALU.mult)
            t = tt("V", [t], yG[:, m, :].rearrange("p (k j) -> p j k", j=8), b1.ap.rearrange("p (j k) -> p j k", j=8),
                   yT[:, m, :].rearrange("p (j k) -> p j k", j=8), ALU.mult)
            b1.free = [t]
            t_ys.append(t)
        bG.free = [t_gl]

        MG = view(zone, 16384, 8, 512)
        t_mg = []
        for m in range(8):
            t_mg.append(merge(A["mg2"], m, [(0, hk, 8), (1024, hk, 8), (2048, lambda k: yfT[:, k, :], 4),
                                            (2560, lambda k: yG[:, k, :], 4)], [t_h, t_yf, t_ys, t_S, t_y], MG[:, m, :], allb, TM2, 3072))
        t_x3, t_last = residual(A["wo2"], lambda k: MG[:, k, :], t_mg)

        XN = view(zone, 0, 4, 1024)
        t_row = rowload("gf", [t_last, t_xb], s_row)
        t_xn = normed(X, [t_x3, t_last], XN)
        t_hn = []
        for i in range(4):
            t_hn.append(tt("V", [t_xn, t_row], XN[:, i, :], XN[:, i, :], row, ALU.mult))
        s_hn = sem("s_hn")
        t_hnd = Q.dma("A", [t_hn], hn_d.rearrange("(i p) d -> p i d", p=P), XN, s_hn)
        t_h = transposed(XN, [t_hn], H, None, allb, [t_last])
        rw = RW.rearrange("p (a b) -> p a b", a=8)
        z = [4096]

        def zl(*shape):
            n = 1
            for d in shape:
                n *= d
            a = view(zone, z[0], *shape)
            z[0] += n
            return a

        LG = zl(4, 72)
        pb, bw = allb.take()
        for i in range(4):
            for k in range(8):
                t = mm([t_h, bw, t_c], pb.ap[:, 72 * i:72 * i + 72], H[:, k, 128 * i:128 * i + 128], rw[:, k, :], k == 0, k == 7, sig=k == 7)
        t = tt("V", [t, t_last], LG, pb.ap[:, 0:288].rearrange("p (a b) -> p a b", a=4), bc(RB, 1, 4), ALU.add)
        pb.free = [t]
        t_lg = t
        mx8 = zl(4, 8)
        ix8 = zl(4, 8)
        for i in range(4):
            t = Q.add("V", [t_lg], lambda eng, i=i: eng.max(mx8[:, i, :], LG[:, i, 0:8]))
            t = Q.add("V", [t], lambda eng, i=i: eng.max_index(ix8.bitcast(U32)[:, i, :], mx8[:, i, :], LG[:, i, 0:8]))
        gi = zl(4)
        t = cp("V", [t], gi, ix8.bitcast(U32)[:, :, 0])
        pg = zl(4)
        e8 = zl(4, 8)
        ta = tt("V", [t], e8, LG[:, :, 0:8], bc(mx8[:, :, 0], 2, 8), ALU.subtract)
        ta = act([ta], e8, e8, ACT.Exp)
        ta = red([ta], pg, e8, ALU.add)
        t_pg = rcp([ta], pg, pg)
        oh = zl(4, 8)
        t = tt("V", [t_pg], oh, bc(ck("iota")[:, 0:8], 1, 4), bc(gi, 2, 8), ALU.is_equal)
        le = zl(4, 8, 8)
        for i in range(4):
            t = tt("V", [t], le[:, i, :, :], LG[:, i, 8:72].rearrange("p (g e) -> p g e", g=8), bc(oh[:, i, :], 2, 8), ALU.mult)
        es = zl(4, 8)
        for i in range(4):
            t = red([t], es[:, i, :], le[:, i, :, :].rearrange("p g e -> p e g"), ALU.add)
        m2 = zl(4, 8)
        i2 = zl(4, 8)
        for i in range(4):
            t = Q.add("V", [t], lambda eng, i=i: eng.max(m2[:, i, :], es[:, i, :]))
            t = Q.add("V", [t], lambda eng, i=i: eng.max_index(i2.bitcast(U32)[:, i, :], m2[:, i, :], es[:, i, :]))
        EX = zl(2, 4)
        WT = zl(2, 4)
        for c in range(2):
            t = cp("V", [t], EX[:, c, :], i2.bitcast(U32)[:, :, c])
            t = stt([t], EX[:, c, :], gi, 8.0, EX[:, c, :], ALU.mult, ALU.add)
        e1 = zl(4)
        t = tt("V", [t], e1, m2[:, :, 1], m2[:, :, 0], ALU.subtract)
        t = act([t], e1, e1, ACT.Exp)
        dn = zl(4)
        t = ts("V", [t], dn, e1, 1.0, None, ALU.add)
        t = rcp([t], dn, dn)
        t = tt("V", [t], WT[:, 0, :], dn, pg, ALU.mult)
        t = tt("V", [t], WT[:, 1, :], WT[:, 0, :], e1, ALU.mult)
        E = zl(2, 4, 64)
        for c in range(2):
            t = tt("V", [t], E[:, c, :, :], bc(ck("iota")[:, 0:64], 1, 4), bc(EX[:, c, :], 2, 64), ALU.is_equal)
        ES = zl(4, 64)
        t = tt("V", [t], ES, E[:, 0, :, :], E[:, 1, :, :], ALU.add)
        pb, bw = allb.take()
        for i in range(4):
            for j in range(i + 1):
                tp = mm([t, bw], pb.ap[:, 64 * i:64 * i + 64], ck("tri") if j == i else ck("ones"), ES[:, j, :], j == 0, j == i)
        for j in range(4):
            tp = mm([], pb.ap[:, 256:320], ck("ones"), ES[:, j, :], j == 0, j == 3, sig=j == 3)
        RK = zl(2, 4)
        rt = zl(4, 64)
        for c in range(2):
            t = tt("V", [tp, t], rt, E[:, c, :, :], pb.ap[:, 0:256].rearrange("p (a b) -> p a b", a=4), ALU.mult)
            t = red([t], RK[:, c, :], rt, ALU.add)
        cnt = zl(1)
        t = red([t], cnt, pb.ap[:, 256:320], ALU.max)
        pb.free = [t]
        NR = zl(1).bitcast(I32)
        sh = CAP.bit_length() - 1
        t = ts("V", [t], cnt, cnt, float(CAP - 1), None, ALU.add)
        t = cp("V", [t], NR, cnt)
        t_nr = ts("V", [t], NR, NR, sh, None, ALU.logical_shift_right)
        EI = zl(2, 4).bitcast(I32)
        HI = zl(2, 4)
        LO = zl(2, 4)
        tI = zl(2, 4).bitcast(I32)
        t = cp("V", [t_nr], EI, EX)
        t = ts("V", [t], tI, EI, 1, None, ALU.logical_shift_right)
        t = cp("V", [t], HI, tI)
        t = ts("V", [t], tI, EI, 1, None, ALU.bitwise_and)
        t = cp("V", [t], LO, tI)
        t = ts("V", [t], LO, LO, 64.0, None, ALU.mult)
        t_route = t

        RR = zl(2, 4)
        OK = zl(2, 4)
        o2 = zl(2, 4)
        AM = zl(2, 4, 128)
        BM = zl(2, 4, 32)
        SLf = zl(2, 4)
        SL = zl(2, 4).bitcast(I32)
        TABr = zl(32)
        TAB = TABr.bitcast(I32)
        WR_ = zl(2, 4)
        OFF = zl(1)
        IDX = zl(1).bitcast(I32)
        XGb = [Buf(zl(1024)) for _ in range(2)]
        XTb = [Buf(zl(8, 128)) for _ in range(2)]
        ATb = [Buf(zl(512)) for _ in range(2)]
        aTb = [Buf(zl(4, 128)) for _ in range(2)]
        YEb = [Buf(zl(1024)) for _ in range(2)]
        YGb = [Buf(zl(1024)) for _ in range(2)]
        ring0 = z[0]
        nring = (24576 - ring0) // 4096
        t_off = Q.memset("V", [t_route], OFF, 0.0)

        def plan(Q, w, bank):
            t = ts2(Q, w, RR, EXRK, OFF)
            t = Q.ts("V", [t], OK, RR, 0.0, None, ALU.is_ge)
            t = Q.ts("V", [t], o2, RR, float(CAP), None, ALU.is_lt)
            t = Q.tt("V", [t], OK, OK, o2, ALU.mult)
            t = Q.tt("V", [t], RR, RR, OK, ALU.mult)
            t = Q.tt("V", [t], WR_, WT, OK, ALU.mult)
            t = Q.stt([t], SLf, EX, 64.0, RR, ALU.mult, ALU.add)
            t_sl = Q.cp("V", [t], SL, SLf)
            t = Q.tt("V", [t_sl], o2, LO, RR, ALU.add)
            for c in range(2):
                t = Q.tt("V", [t], AM[:, c, :, :], bc(ck("iota"), 1, 4), bc(o2[:, c, :], 2, 128), ALU.is_equal)
                t = Q.tt("V", [t], BM[:, c, :, :], bc(ck("iota")[:, 0:32], 1, 4), bc(HI[:, c, :], 2, 32), ALU.is_equal)
            t = Q.tt("V", [t], OK, OK, bc(ck("tok"), 1, 2), ALU.mult)
            for c in range(2):
                t = Q.tt("V", [t], BM[:, c, :, :], BM[:, c, :, :], bc(OK[:, c, :], 2, 32), ALU.mult)
            for n in range(8):
                tp = Q.mm([t, w], bank.ap[:, 0:32], AM[:, n // 4, n % 4, :], BM[:, n // 4, n % 4, :], n == 0, n == 7, sig=n == 7)
            t_tab = Q.cp("V", [tp], TAB, bank.ap[:, 0:32])
            return t_tab, t_sl, t

        def ts2(Q, w, out, a, off):
            return Q.ts("V", w, out, a, off, None, ALU.subtract)
        EXRK = RK

        def expert_pair(Q, q, idx, w_idx, wsrc, wload, mb, xg, xt, at_, aT, ye, gsem, ysem, y_out, tw_extra=()):
            g, gw = xg, xg.take()
            tg = Q.gather([gw, w_idx], g.ap, hn_d, idx, gsem)
            x, xw = xt, xt.take()
            tx = []
            for hf in range(2):
                b, bw = mb.take()
                for k in range(4):
                    kk = 4 * hf + k
                    t = Q.tr([tg, bw], b.ap[:, 128 * k:128 * k + 128], g.ap.rearrange("p (a b) -> p b a", b=8)[:, kk, :], ident, sig=k == 3)
                t2 = Q.cp("AV"[hf], [t, xw], x.ap[:, 4 * hf:4 * hf + 4, :], b.ap.rearrange("p (a b) -> p a b", a=4))
                b.free = [t2]
                tx.append(t2)
            g.free = [t]
            res = []
            for mat in range(2):
                s0, w0 = wload(mat, 0)
                s1, w1 = wload(mat, 1)
                pb, bw = mb.take()
                for k in range(8):
                    for e in range(2):
                        s, w_ = ((s0, w0), (s1, w1))[e]
                        t = Q.mm([tx, w_, bw], pb.ap[64 * e:64 * e + 64, :], x.ap[:, k, 64 * e:64 * e + 64], s.ap[:, 512 * k:512 * k + 512],
                                 k == 0, k == 7, sig=k == 7)
                s0.free = [t]
                s1.free = [t]
                res.append((pb, t))
            x.free = [t]
            a, aw = at_, at_.take()
            (pg_, tg_), (pu_, tu_) = res
            t = Q.act([tg_, aw], a.ap, pg_.ap, ACT.Tanh, scale=0.5)
            t = Q.stt([t], a.ap, a.ap, 1.0, pg_.ap, ALU.add, ALU.mult)
            pg_.free = [t]
            t = Q.stt([t, tu_], a.ap, a.ap, 0.5, pu_.ap, ALU.mult, ALU.mult)
            pu_.free = [t]
            b, bw = mb.take()
            for k in range(4):
                tt_ = Q.tr([t, bw], b.ap[:, 128 * k:128 * k + 128], a.ap.rearrange("p (a b) -> p b a", b=4)[:, k, :], ident, sig=k == 3)
            a.free = [tt_]
            c, cw_ = aT, aT.take()
            t_a = Q.cp("A", [tt_, cw_], c.ap, b.ap.rearrange("p (a b) -> p a b", a=4))
            b.free = [t_a]
            s0, w0 = wload(2, 0)
            s1, w1 = wload(2, 1)
            y, yw = ye, ye.take()
            ty = []
            for nh in range(2):
                pb, bw = mb.take()
                for k in range(4):
                    for e in range(2):
                        s, w_ = ((s0, w0), (s1, w1))[e]
                        t = Q.mm([t_a, w_, bw], pb.ap[64 * e:64 * e + 64, :], c.ap[:, k, 64 * e:64 * e + 64],
                                 s.ap[:, 1024 * k + 512 * nh:1024 * k + 512 * nh + 512], k == 0, k == 3, sig=k == 3)
                t2 = Q.cp("VA"[nh], [t, yw], y.ap[:, 512 * nh:512 * nh + 512], pb.ap)
                pb.free = [t2]
                ty.append(t2)
            s0.free = [t]
            s1.free = [t]
            c.free = [t]
            td = Q.dma("A", ty, y_out, y.ap, ysem)
            y.free = [td]
            return td

        def combine(Q, w, gsems, bufs):
            out_t = []
            for n in range(8):
                i, c = n // 2, n % 2
                b = bufs[n % 2]
                t = Q.gather([w, b.take()], b.ap, y_d, SL[:, c, i:i + 1], gsems[n % 2])
                t = Q.stt([t] + out_t[-1:], X[:, i, :], b.ap, WR_[:, c, i:i + 1], X[:, i, :], ALU.mult, ALU.add)
                b.free = [t]
                out_t.append(t)
            return out_t

        t_tab, t_sl, t_pl = plan(Q, [t_off, t_last, t_h, allb.bufs[0].free], allb.bufs[0])
        allb.bufs[0].free = [t_tab]

        gsem = [sem("s_ga"), sem("s_gb")]
        ysem = [sem("s_ya"), sem("s_yb")]
        csem = [sem("s_ca"), sem("s_cb")]
        extra = [Buf(view(zone, ring0 + 4096 * q, 4096), sem(f"wx{q}")) for q in range(nring)]
        for b in extra:
            b.free = [t_last, t_h]
        start = WQ.i
        MQ = Ring(WR[start:] + WR[:start] + extra)

        EW = [A["eg"].rearrange("e (p t) n -> e p (t n)", p=P), A["eu"].rearrange("e (p t) n -> e p (t n)", p=P),
              A["ed"].rearrange("e (p t) n -> e p (t n)", p=P)]
        mb = Ring(banks)
        ends = []
        for q in range(32):
            def wload(mat, e, q=q):
                b, w = MQ.take()
                return b, Q.dma("S", w, b.ap, EW[mat][2 * q + e], b.sem)
            ends.append(expert_pair(Q, q, TAB[:, q:q + 1], [t_tab, t_hnd], None, wload, mb, XGb[q % 2], XTb[q % 2], ATb[q % 2], aTb[q % 2], YEb[q % 2],
                                    gsem[q % 2], ysem[q % 2], y_d[128 * q:128 * q + 128, :]))
        t_cb = combine(Q, [ends], csem, YGb)

        r_sems = {e: sem("r" + e) for e in "TVAG"}
        r_dma = [sem(f"r_d{q}") for q in range(6)]
        r_g = sem("r_g")
        r_y = sem("r_y")
        r_c = [sem("r_ca"), sem("r_cb")]
        meet_in = sem("meet")
        go = {e: sem("go" + e) for e in "TVAG"}
        clear = list(r_sems.values()) + r_dma + [r_g, r_y] + r_c

        def part(build):
            q2 = Queue(r_sems)
            for b in banks + XGb + XTb + ATb + aTb + YEb + YGb + WR + extra:
                b.free = []
            build(q2)
            for e in "TVAG":
                n = q2.n.get(r_sems[e].name, 0)
                if n:
                    q2.wait(e, [(r_sems[e], n)])
            return q2

        def more(q2):
            t = q2.ts("V", [], OFF, OFF, float(CAP), None, ALU.add)
            plan(q2, [t], banks[0])

        def pair_part(q2, reg):
            def wload(mat, e):
                n = 2 * mat + e
                b = (WR + extra)[n % (4 + nring)]
                w = b.take()
                d = r_dma[n]

                def go_(eng):
                    eng.dma_start(b.ap, EWd[mat][bass.ds(reg["S"] * 2 + e, 1), :, :].rearrange("a p f -> p (a f)")).then_inc(d, 16)
                q2.wait("S", w)
                q2.n[d.name] = 16
                q2.raw("S", go_)
                return b, (d, 16)
            t = q2.add("V", [], lambda eng: eng.tensor_copy(IDX, TAB[:, bass.ds(reg["V"], 1)]))

            def st(eng):
                eng.dma_start(y_d.rearrange("(q p) d -> q p d", p=P)[bass.ds(reg["A"], 1), :, :].rearrange("a p d -> p (a d)"), YEb[0].ap).then_inc(r_y, 16)
            expert_pair_dyn(q2, t, wload, st)

        EWd = EW

        def expert_pair_dyn(q2, t_idx, wload, st):
            class Store:
                pass
            orig = q2.dma

            def dma(e, w, out, in_, sem_):
                q2.wait(e, w)
                q2.n[sem_.name] = q2.n.get(sem_.name, 0) + 16
                q2.raw(e, st)
                return (sem_, q2.n[sem_.name])
            q2.dma = dma
            t = expert_pair(q2, 0, IDX, [t_idx], None, wload, Ring(banks), XGb[0], XTb[0], ATb[0], aTb[0], YEb[0], r_g, r_y, None)
            q2.dma = orig
            q2.wait("A", [t])

        def tail(q2):
            ends2 = combine(q2, [], r_c, YGb)
            q2.wait("V", ends2)

        reg = {}
        P_more = part(more)
        P_pair = part(lambda q2: pair_part(q2, reg))
        P_tail = part(tail)

        s_fin = sem("s_fin")
        t_row = Q.dma("A", [t_hn], row, A["fn2"].partition_broadcast(P), s_row)

        QF = Queue({e: sem("f" + e) for e in "TVAG"})

        def last_norm():
            Z = view(zone, 0, 4, 1024)
            v = view(zone, 4096, 4)
            s4 = view(zone, 4100, 4)
            r4 = view(zone, 4104, 4)
            t = None
            for i in range(4):
                t = QF.act([t], Z[:, i, :], X[:, i, :], ACT.Square, acc=v[:, i:i + 1])
            t = QF.ts("V", [t], v, v, 1.0 / 1024, 1e-6, ALU.mult, ALU.add)
            t = QF.act([t], s4, v, ACT.Sqrt)
            t = QF.rcp([t], r4, s4)
            t = QF.tt("V", [t], s4, r4, r4, ALU.mult)
            t = QF.tt("V", [t], s4, s4, v, ALU.mult)
            t = QF.ts("V", [t], s4, s4, -0.5, 1.5, ALU.mult, ALU.add)
            t = QF.tt("V", [t], r4, r4, s4, ALU.mult)
            td = []
            for i in range(4):
                t1 = QF.stt([t], Z[:, i, :], X[:, i, :], r4[:, i:i + 1], row, ALU.mult, ALU.mult)
                td.append(QF.dma("S", [t1], out[128 * i:128 * i + 128, :], Z[:, i, :], s_fin))
            QF.wait("S", td[-1:])

        last_norm()

        def meet(eng, e, first=False):
            if e == "S":
                eng.wait_ge(meet_in, 4)
                eng.sem_clear(meet_in)
                for s in clear:
                    eng.sem_clear(s)
                for k in "TVAG":
                    eng.sem_inc(go[k], 1)
            else:
                eng.sem_inc(meet_in, 1)
                eng.wait_ge(go[e], 1)
                eng.sem_clear(go[e])

        Q.wait("V", [t_cb])
        Q.wait("A", [t_row, ends])
        for e in "TVAGS":
            Q.wait(e, [t_nr])
            if e != "V":
                Q.wait(e, [t_cb[-1]])
        with nc.Block() as block:
            for e, on in (("S", block.sync), ("T", block.tensor), ("V", block.vector), ("A", block.scalar), ("G", block.gpsimd)):
                @on
                def _(eng, e=e):
                    for f in Q.q[e]:
                        f(eng)
                    rounds = eng.value_load(NR[0:1, 0:1], min_val=1, max_val=512 // CAP)
                    r = eng.alloc_register("round" + e)
                    eng.reg_mov(r, 1)
                    meet(eng, e)
                    with eng.While(lambda: eng.snap(r) < rounds):
                        for f in P_more.q[e]:
                            f(eng)
                        meet(eng, e)
                        k = eng.alloc_register("pair" + e)
                        eng.reg_mov(k, 0)
                        with eng.While(lambda: eng.snap(k) < 32):
                            reg[e] = eng.snap(k, min_val=0, max_val=31)
                            for f in P_pair.q[e]:
                                f(eng)
                            meet(eng, e)
                            eng.reg_add(k, k, 1)
                        for f in P_tail.q[e]:
                            f(eng)
                        meet(eng, e)
                        eng.reg_add(r, r, 1)
                    for f in QF.q[e]:
                        f(eng)


def host(inp):
    g = {k: np.asarray(v) for k, v in inp.items()}
    w = g["w_in"][0]
    off = np.cumsum([0, 512, 128, 128, 128, 128, 128, 128, 24, 1024, 1024, 1024, 1024])
    cols = []
    for j in range(4):
        cols += [np.arange(64 * j, 64 * j + 64), np.arange(64 * (j + 4), 64 * (j + 4) + 64)]
    cols += [np.arange(off[3], off[3] + 128), np.arange(off[5], off[5] + 128)]
    for b in (off[1], off[2]):
        for q in range(2):
            cols += [np.arange(b + 64 * q, b + 64 * q + 64)] * 2
    for half in range(2):
        for b in (off[8], off[9]):
            cols += [np.arange(b + 512 * half, b + 512 * half + 512)]
    cols = np.concatenate(cols)

    def ft(a):
        K, M = a.shape
        return np.ascontiguousarray(a.reshape(K // 128, 128, M // 128, 128).transpose(1, 2, 0, 3))

    def rows(a):
        K, N = a.shape
        return np.ascontiguousarray(a.reshape(K // 128, 128, N).transpose(1, 0, 2).reshape(128, -1))

    def halves(a):
        return np.concatenate([rows(a[:, :512]), rows(a[:, 512:])], 1)

    def pf(a):
        return a.reshape(-1, 128).T

    o = {"x": g["x"][0]}
    o["winF"] = ft(w[:, cols]).reshape(128, -1)
    o["winN"] = rows(w[:, np.concatenate([np.arange(off[4], off[4] + 128), np.arange(off[6], off[6] + 128), np.arange(off[7], off[7] + 24)])])
    heads = np.concatenate([np.arange(64 * hd, 64 * hd + 64) for j in range(4) for hd in (j, j + 4)])
    o["mg1"] = np.concatenate([ft(w[:, off[10]:off[11]]).reshape(128, 8, -1), ft(w[:, off[11]:off[12]]).reshape(128, 8, -1),
                               ft(g["w_up_attn"][0][heads]).reshape(128, 8, -1), ft(g["w_up_rnn"][0]).reshape(128, 8, -1)], 2).reshape(128, -1)
    o["wo1"] = halves(g["w_out"][0])
    o["m1"] = ft(g["mlp_w1"][0]).reshape(128, -1)
    o["m2"] = rows(g["mlp_w2"][0])
    lru = np.zeros((128, 2, 8, 128), np.float32)
    for q, n in enumerate(("lru_w_a", "lru_w_i")):
        a = g[n][0].reshape(8, 2, 64, 64)
        for b in range(2):
            lru[64 * b:64 * b + 64, q, :, 64 * b:64 * b + 64] = a[:, b].transpose(1, 0, 2)
    o["lru"] = lru
    o["cw1"] = np.stack([rows(g["cmp_k_w1"][0]), rows(g["cmp_v_w1"][0])], 1)
    sm = np.zeros((128, SM_N), np.float32)

    def put(n, a):
        c, k = SM_COLS[n]
        sm[:, c:c + k] = a.reshape(128, k)

    put("n1", pf(g["norm1_w"]))
    put("n2", pf(g["norm2_w"]))
    put("mix", pf(g["mix_norm_g_2"]))
    put("cw", np.concatenate([pf(g["conv_w"][0][i]) for i in range(4)], 1))
    put("cb", pf(g["conv_b"]))
    put("ba", pf(g["lru_b_a"]))
    put("bi", pf(g["lru_b_i"]))
    put("lam", pf(g["lru_lambda"]))
    put("dsk", pf(g["ssm_D_2"]))
    put("are", g["ssm_A_re_2"][0].transpose(0, 2, 1))
    put("aim", g["ssm_A_im_2"][0].transpose(0, 2, 1))
    put("ldt", np.repeat(g["ssm_log_dt_2"][0][:, None, :], 64, 1))
    put("pk", g["cmp_pos_k"][0].reshape(16, 128).T)
    put("pv", g["cmp_pos_v"][0].reshape(16, 128).T)
    put("kw2", g["cmp_k_w2"][0].reshape(2, 128, 64).transpose(1, 0, 2))
    put("vw2", g["cmp_v_w2"][0].reshape(2, 128, 64).transpose(1, 0, 2))
    o["sm"] = sm
    ckc = np.zeros((128, CK_N), np.float32)

    def putc(n, a):
        c, k = CK_COLS[n]
        ckc[:, c:c + k] = a.reshape(128, k)

    r = np.arange(128)
    putc("ident", np.eye(128))
    putc("neg", np.where(r[None, :] > r[:, None], -1e30, 0.0))
    tq = r[:, None] + 128 * np.arange(4)[None, :]
    ok = (16 * np.arange(31) + 31)[None, None, :] <= tq[:, :, None]
    putc("cneg", np.where(ok, 0.0, -1e30))
    putc("c01", np.where(ok, 1.0, 0.0))
    putc("tri", (r[:, None] < r[None, :]).astype(np.float32))
    putc("ones", np.ones((128, 128)))
    putc("iota", np.tile(r[None, :], (128, 1)))
    putc("tok", tq)
    ang = 2 * np.pi * (np.outer(r, r) % 128) / 128
    putc("cs", np.concatenate([np.cos(ang), np.sin(ang)], 1) / 256)
    o["ck"] = ckc
    o["fn1"], o["gf"], o["fn2"] = g["final_norm_w"], g["ffn_norm_g_2"][0], g["final_norm_g_2"]

    def nb(a):
        return a.reshape(128, 512)

    o["bb"] = np.concatenate([nb(g["ssm_B_%s_2" % n][0].transpose(0, 2, 1, 3)) for n in ("re", "im")], 1)
    o["cc"] = np.concatenate([nb(g["ssm_C_%s_2" % n][0].transpose(0, 3, 1, 2)) for n in ("re", "im")], 1)
    w2 = g["w_in_2"][0]
    o["z2"] = ft(w2[:, :1024]).reshape(128, -1)
    o["mg2"] = np.concatenate([ft(w2[:, 1024:2048]).reshape(128, 8, -1), ft(w2[:, 2048:]).reshape(128, 8, -1),
                               ft(g["w_fourier_out_2"][0]).reshape(128, 8, -1), ft(g["w_ssm_out_2"][0]).reshape(128, 8, -1)], 2).reshape(128, -1)
    o["wo2"] = halves(g["w_out_2"][0])
    o["glu"] = ft(g["ssm_w_glu_2"][0]).reshape(128, -1)
    n = np.arange(512)
    a5 = 2 * np.pi * (np.outer(n, n) % 512) / 512
    o["dft"] = np.concatenate([rows(np.cos(a5)), rows(-np.sin(a5))], 1).astype(np.float32)
    o["eg"], o["eu"], o["ed"] = (g["expert_w_%s_2" % n][0] for n in ("gate", "up", "down"))
    o["rw"] = rows(np.concatenate([g["router_group_w_2"][0], g["router_expert_w_2"][0]], 1))
    o["rb"] = np.concatenate([g["router_group_b_2"][0], g["router_expert_b_2"][0]])
    return {k: np.ascontiguousarray(v) for k, v in o.items()}


_INS = ["x", "sm", "ck", "rw", "rb", "winF", "winN", "lru", "cw1", "mg1", "wo1", "m1", "m2", "fn1", "bb", "cc", "z2", "dft", "glu",
        "mg2", "wo2", "gf", "fn2", "eg", "eu", "ed"]


def kernel(**inputs):
    import concourse.bacc as bacc
    from concourse.bass_utils import run_bass_kernel_spmd

    arrays = host(inputs)
    nc = bacc.Bacc("TRN2", target_bir_lowering=False, num_devices=1)
    A = {n: nc.dram_tensor("in_" + n, arrays[n].shape, F32, kind="ExternalInput").ap() for n in _INS}
    out = nc.dram_tensor("out_0", (512, 1024), F32, kind="ExternalOutput").ap()
    program(nc, A, out)
    r = run_bass_kernel_spmd(nc, [{"in_" + n: arrays[n] for n in _INS}], core_ids=[0])
    return r.results[0]["out_0"].reshape(1, 512, 1024)
```

```python
import math
from contextlib import ExitStack

import numpy as np
import concourse.bass as bass
from concourse import mybir

F32 = mybir.dt.float32
I32 = mybir.dt.int32
U32 = mybir.dt.uint32
ACT = mybir.ActivationFunctionType
ALU = mybir.AluOpType
AX = mybir.AxisListType

P = 128
CAP = 64

SM_COLS = {}


def _cols(table, spec):
    at = 0
    for name, n in spec:
        table[name] = (at, n)
        at += n
    return at


SM_N = _cols(SM_COLS, [("n1", 8), ("n2", 8), ("mix", 8), ("cw", 32), ("cb", 8), ("ba", 8), ("bi", 8),
                       ("lam", 8), ("dsk", 4), ("are", 32), ("aim", 32), ("ldt", 32), ("pk", 16), ("pv", 16),
                       ("kw2", 128), ("vw2", 128)])
CK_COLS = {}
CK_N = _cols(CK_COLS, [("ident", 128), ("neg", 128), ("cneg", 124), ("c01", 124), ("tri", 128), ("ones", 128),
                       ("iota", 128), ("tok", 4), ("cs", 256)])


class Buf:

    def __init__(self, ap, sem=None):
        self.ap = ap
        self.sem = sem
        self.free = []

    def take(self):
        assert self.free is not None, "taken while in use"
        w, self.free = self.free, None
        return w


class Ring:
    def __init__(self, bufs):
        self.bufs = bufs
        self.i = 0

    def take(self):
        b = self.bufs[self.i]
        self.i = (self.i + 1) % len(self.bufs)
        return b, b.take()


class Queue:

    def __init__(self, sems):
        self.q = {e: [] for e in "TVAGS"}
        self.sem = sems
        self.n = {}
        self.seen = {}

    def wait(self, e, toks):
        for t in toks:
            if t is None:
                continue
            if isinstance(t, list):
                self.wait(e, t)
                continue
            sem, v = t
            if self.seen.get((e, sem.name), 0) < v:
                self.seen[(e, sem.name)] = v
                self.q[e].append(lambda eng, s=sem, v=v: eng.wait_ge(s, v))

    def add(self, e, w, fn, sig=True):
        self.wait(e, w)
        if not sig:
            self.q[e].append(fn)
            return None
        s = self.sem[e]
        self.n[s.name] = self.n.get(s.name, 0) + 1
        self.q[e].append(lambda eng, f=fn, s=s: f(eng).then_inc(s, 1))
        return (s, self.n[s.name])

    def raw(self, e, fn):
        self.q[e].append(fn)

    def dma(self, e, w, out, in_, sem):
        self.wait(e, w)
        self.n[sem.name] = self.n.get(sem.name, 0) + 16
        self.q[e].append(lambda eng: eng.dma_start(out, in_).then_inc(sem, 16))
        return (sem, self.n[sem.name])

    def gather(self, w, out, in_, idx, sem):
        self.wait("G", w)
        self.n[sem.name] = self.n.get(sem.name, 0) + 16
        self.q["G"].append(lambda eng: eng.indirect_dma_start(
            out=out, out_offset=None, in_=in_,
            in_offset=bass.IndirectOffsetOnAxis(ap=idx, axis=0)).then_inc(sem, 16))
        return (sem, self.n[sem.name])

    def mm(self, w, out, lhsT, rhs, start, stop, sig=False):
        return self.add("T", w, lambda eng: eng.matmul(out, lhsT, rhs, start=start, stop=stop), sig)

    def tr(self, w, out, in_, ident, sig=False):
        return self.add("T", w, lambda eng: eng.transpose(out, in_, ident), sig)

    def act(self, w, out, in_, func, bias=0.0, scale=1.0, acc=None):
        if acc is None:
            return self.add("A", w, lambda eng: eng.activation(out, in_, func, bias=bias, scale=scale))
        return self.add("A", w, lambda eng: eng.activation(out, in_, func, bias=bias, scale=scale, accum_out=acc))

    def tt(self, e, w, out, a, b, op):
        return self.add(e, w, lambda eng: eng.tensor_tensor(out, a, b, op))

    def ts(self, e, w, out, a, s1, s2, op0, op1=None):
        if op1 is None:
            return self.add(e, w, lambda eng: eng.tensor_scalar(out, a, s1, None, op0))
        return self.add(e, w, lambda eng: eng.tensor_scalar(out, a, s1, s2, op0, op1))

    def stt(self, w, out, a, s, b, op0, op1):
        return self.add("V", w, lambda eng: eng.scalar_tensor_tensor(out, a, s, b, op0, op1))

    def cp(self, e, w, out, a):
        if e == "A":
            return self.act(w, out, a, ACT.Copy)
        return self.add(e, w, lambda eng: eng.tensor_copy(out, a))

    def red(self, w, out, a, op):
        return self.add("V", w, lambda eng: eng.tensor_reduce(out, a, op=op, axis=AX.X))

    def scan(self, w, out, a, b):
        return self.add("V", w, lambda eng: eng.tensor_tensor_scan(out, a, b, 0.0, ALU.mult, ALU.add))

    def rcp(self, w, out, a):
        return self.add("V", w, lambda eng: eng.reciprocal(out, a))

    def memset(self, e, w, out, v):
        return self.add(e, w, lambda eng: eng.memset(out, v))


def bc(ap, axis, n):
    a = ap.unsqueeze(axis)
    shape = list(a.shape)
    shape[axis] = n
    return a.to_broadcast(shape)


def weave(a, b):
    for n in a:
        for _ in range(n):
            next(b, None)
    run(b)


def run(g):
    for _ in g:
        pass


def program(nc, A, out):
    ctx = ExitStack()
    with ctx:
        SB = ctx.enter_context(nc.sbuf_tensor("sb", [P, 53000], F32))
        PS = ctx.enter_context(nc.psum_tensor("ps", [P, 8 * 512], F32))
        names = {}

        def sem(n):
            names[n] = ctx.enter_context(nc.semaphore(n))
            return names[n]

        def dram(n, shape):
            return nc.dram_tensor(n, shape, F32).ap()

        hn_d = dram("hn_d", (512, 1024))
        y_d = dram("y_d", (4096, 1024))
        u_d = dram("u_d", (512, 512))
        yo_d = dram("yo_d", (512, 512))
        mbr_d = dram("mbr_d", (P, 32, 128))
        mbi_d = dram("mbi_d", (P, 32, 128))
        mcr_d = dram("mcr_d", (P, 32, 128))
        mci_d = dram("mci_d", (P, 32, 128))

        engine_sems = {e: sem("s" + e) for e in "TVAG"}
        Q = Queue(engine_sems)
        mm, tr, act, tt, ts, stt, cp, red, rcp = Q.mm, Q.tr, Q.act, Q.tt, Q.ts, Q.stt, Q.cp, Q.red, Q.rcp

        at = [0]

        def al(*shape):
            n = 1
            for d in shape:
                n *= d
            a = SB[:, at[0]:at[0] + n]
            at[0] += n
            assert at[0] <= 53000, at[0]
            if len(shape) == 2:
                a = a.rearrange("p (a b) -> p a b", b=shape[1])
            elif len(shape) == 3:
                a = a.rearrange("p (a b c) -> p a b c", b=shape[1], c=shape[2])
            return a

        def view(base, off, *shape):
            n = 1
            for d in shape:
                n *= d
            a = base[:, off:off + n]
            if len(shape) == 2:
                a = a.rearrange("p (a b) -> p a b", b=shape[1])
            elif len(shape) == 3:
                a = a.rearrange("p (a b c) -> p a b c", b=shape[1], c=shape[2])
            return a

        X = al(4, 1024)
        SMt = al(SM_N)
        CKt = al(CK_N)
        misc = al(400)
        RW = al(8 * 72)
        RB = al(72)
        H = al(8, 512)
        WR = [Buf(al(4096), sem(f"w{i}")) for i in range(4)]
        zone = al(53000 - at[0])
        ZN = zone.shape[1]
        zat = [0]

        def zal(*shape):
            n = 1
            for d in shape:
                n *= d
            a = view(zone, zat[0], *shape)
            zat[0] += n
            assert zat[0] <= ZN, (zat[0], ZN)
            return a

        banks = [Buf(PS[:, 512 * i:512 * i + 512]) for i in range(8)]

        def sm(n):
            a, k = SM_COLS[n]
            return SMt[:, a:a + k]

        def ck(n):
            a, k = CK_COLS[n]
            return CKt[:, a:a + k]

        mi = [0]

        def small(n):
            a = misc[:, mi[0]:mi[0] + n]
            mi[0] += n
            assert mi[0] <= 400
            return a

        ident = ck("ident")
        s_c = sem("s_c")
        s_x = sem("s_x")
        s_lru = sem("s_lru")
        t_x = [Q.dma("S", [], X[:, i, :], A["x"][128 * i:128 * i + 128, :], sem(f"s_x{i}")) for i in range(4)]
        Q.dma("A", [], SMt, A["sm"], s_c)
        t_c = Q.dma("A", [], CKt, A["ck"], s_c)

        WQ = Ring(WR)

        def weights(src, n=4096):
            b, w = WQ.take()
            t = Q.dma("S", w, b.ap[:, 0:n], src, b.sem)
            return b, t

        def rstd_of(v, n, w, eps=1e-6):
            s = small(n)
            r = small(n)
            t = ts("V", w, v, v, 1.0 / 1024, eps, ALU.mult, ALU.add)
            ta = act([t], s, v, ACT.Sqrt)
            t = rcp([ta], r, s)
            t = tt("V", [t], s, r, r, ALU.mult)
            t = tt("V", [t], s, s, v, ALU.mult)
            t = ts("V", [t], s, s, -0.5, 1.5, ALU.mult, ALU.add)
            t = tt("V", [t], r, r, s, ALU.mult)
            return r, t

        def normed(xin, w, XN, w_out=None, gain=None, w_gain=None, out=None, scratch=None):
            v = small(4)
            t = act([w[0]], small(1), xin[:, 0, 0:1], ACT.Sqrt, scale=0.0)
            for i in range(4):
                t = act([w[i], t], (XN if scratch is None else scratch)[:, i, :], xin[:, i, :], ACT.Square, acc=v[:, i:i + 1])
            r, t = rstd_of(v, 4, [t])
            t = [t, w_out]
            tk = []
            for i in range(4):
                if gain is not None:
                    tk.append(stt([t, w_gain], out[:, i, :], xin[:, i, :], r[:, i:i + 1], gain, ALU.mult, ALU.mult))
                elif i % 2:
                    tk.append(act([t], XN[:, i, :], xin[:, i, :], ACT.Copy, scale=r[:, i:i + 1]))
                else:
                    tk.append(ts("V", [t], XN[:, i, :], xin[:, i, :], r[:, i:i + 1], None, ALU.mult))
            return tk

        def transposed(XN, w, HT, gain, pr, hw):
            toks = []
            for k in range(8):
                b, bw = pr.take()
                for i in range(4):
                    t = tr([w, bw], b.ap[:, 128 * i:128 * i + 128], XN[:, i, 128 * k:128 * k + 128], ident, sig=i == 3)
                g = gain[:, k:k + 1] if gain is not None else 1.0
                if k % 2:
                    t = act([t, t_c, hw], HT[:, k, :], b.ap, ACT.Copy, scale=g)
                else:
                    t = ts("V", [t, t_c, hw], HT[:, k, :], b.ap, g, None, ALU.mult)
                b.free = [t]
                toks.append(t)
            return toks

        def ftile(pr, wt, rhs, nk, w, last=True):
            b, bw = pr.take()
            t = None
            for k in range(nk):
                t = mm([w, bw], b.ap, wt(k), rhs(k), k == 0, k == nk - 1, sig=k == nk - 1)
            return b, t

        dense = Ring(banks[0:2])
        z0 = zat[0]
        XN = zal(4, 1024)
        T_ = view(zone, z0, 4, 512)
        GX = view(zone, z0 + 2048, 4, 512)
        GR = zal(8, 512)
        qT = zal(4, 512)
        kT = zal(2, 512)
        Vn = zal(4, 256)
        gate = zal(4, 24)
        z1 = zat[0]
        KC = [zal(2, 512), zal(2, 512)]
        BLK = [zal(16, 62), zal(16, 62)]
        PCT = view(zone, z1, 8, 512)
        zat[0] = max(zat[0], z1 + 4096)
        attnT = zal(4, 512)
        PR = [Buf(zal(2, 512)) for _ in range(2)]
        PTR = Ring([Buf(zal(512)) for _ in range(2)])
        XR = Ring([Buf(zal(515)) for _ in range(2)])
        XC = Ring([Buf(zal(512)) for _ in range(2)])
        TMP = Ring([Buf(zal(512)) for _ in range(3)])

        t_xn = normed(X, t_x, XN)
        t_h = transposed(XN, [t_xn, t_c], H, sm("n1"), Ring(banks), [])
        xn_read = t_h

        def hk(k):
            return H[:, k, :]

        halfb = small(16)
        t_hb = ts("V", [t_c], halfb[:, 0:8], sm("ba"), 0.5, None, ALU.mult)
        t_hb = ts("V", [t_hb], halfb[:, 8:16], sm("bi"), 0.5, None, ALU.mult)

        def precise_exp(x, n, w):
            a, b = small(n), small(n)
            t = act(w, a, x, ACT.Tanh, scale=1.0 / 16)
            t = ts("V", [t], b, a, -1.0, 1.0, ALU.mult, ALU.add)
            t = rcp([t], b, b)
            t = stt([t], a, a, 1.0, b, ALU.add, ALU.mult)
            for _ in range(3):
                t = tt("V", [t], a, a, a, ALU.mult)
            return a, t

        sp = small(8)
        nab = small(8)
        t = ts("V", [t_c], nab, sm("lam"), -1.0, None, ALU.mult)
        t = tt("V", [t], nab, nab, sm("lam"), ALU.min)
        ew, t = precise_exp(nab, 8, [t])
        t = ts("V", [t], nab, ew, 2.0, None, ALU.add)
        t = rcp([t], nab, nab)
        t = tt("V", [t], ew, ew, nab, ALU.mult)
        z2 = small(8)
        t = tt("V", [t], z2, ew, ew, ALU.mult)
        t = ts("V", [t], nab, z2, 1.0 / 17, 1.0 / 15, ALU.mult, ALU.add)
        for d in (13, 11, 9, 7, 5, 3, 1):
            t = tt("V", [t], nab, nab, z2, ALU.mult)
            t = ts("V", [t], nab, nab, 1.0 / d, None, ALU.add)
        t = tt("V", [t], nab, nab, ew, ALU.mult)
        t = ts("V", [t], z2, sm("lam"), -1.0, 0.0, ALU.mult, ALU.max)
        t = stt([t], sp, nab, 2.0, z2, ALU.mult, ALU.add)
        m2sp = small(8)
        t_sp = ts("V", [t], m2sp, sp, -2.0, None, ALU.mult)
        tiles = {}
        cur = {}

        def ftiles(src, total):
            state = {"g": -1}

            def get(m):
                g = m // 4
                if g != state["g"]:
                    n = min(4, total - 4 * g)
                    state["b"], state["t"] = weights(src[:, 4096 * g:4096 * g + 1024 * n], 1024 * n)
                    state["g"] = g
                b = state["b"]
                off = (m % 4) * 1024
                return b, state["t"], lambda k: b.ap[:, off + 128 * k:off + 128 * k + 128]
            return get

        getF = ftiles(A["winF"], 26)

        def proj(get, m, rhs, w, pr, total):
            b, t, wt = get(m)
            pb, tm = ftile(pr, wt, rhs, 8, [t, w])
            if m % 4 == 3 or m == total - 1:
                b.free = [tm]
            return pb, tm

        def proj_steps(get, m, total):
            b, tw, wt = get(m)
            pb, bw = dense.take()
            for k in range(8):
                t = mm([tw, t_h, bw], pb.ap, wt(k), hk(k), k == 0, k == 7, sig=k == 7)
                if k % 2 and k < 7:
                    yield
            if m % 4 == 3 or m == total - 1:
                b.free = [t]
            return pb, t

        t_q = []
        for m in range(4):
            pb, t = proj(getF, m, hk, t_h, dense, 26)
            pb.free = [cp("AV"[m % 2], [t], qT[:, m, :], pb.ap)]
            t_q += pb.free
        t_k = []
        for m in range(2):
            pb, t = proj(getF, 4 + m, hk, t_h, dense, 26)
            pb.free = [cp("AV"[m % 2], [t], kT[:, m, :], pb.ap)]
            t_k += pb.free
        t_kc = [[], []]
        for m in range(4):
            pb, t = proj(getF, 6 + m, hk, t_h, dense, 26)
            dst = KC[m // 2][:, m % 2, :]
            ta = cp("A", [t], dst[0:64, :], pb.ap[0:64, :])
            tb = cp("V", [t], dst[64:128, 0:511], pb.ap[64:128, 1:512])
            pb.free = [ta, tb]
            t_kc[m // 2] += [ta, tb]

        bN, tN = weights(A["winN"], 8 * 280)
        wN = view(bN.ap, 0, 8, 280)
        t_v = []
        gz = []
        for i in range(4):
            b, bw = dense.take()
            for k in range(8):
                t = mm([t_h, tN, bw], b.ap[:, 0:280], H[:, k, 128 * i:128 * i + 128], wN[:, k, :], k == 0, k == 7, sig=k == 7)
            ta = cp("V", [t], Vn[:, i, :], b.ap[:, 0:256])
            tb = act([t, ta], gate[:, i, :], b.ap[:, 256:280], ACT.Tanh, scale=0.5)
            b.free = [ta, tb]
            t_v.append(ta)
            gz.append(tb)
        bN.free = [t]
        t_gate = ts("V", gz, gate, gate, 0.5, 0.5, ALU.mult, ALU.add)

        own = [WR[0], WR[3]]
        WQ = Ring([WR[1], WR[2]])
        GT = [view(b.ap, 0, 8, 512) for b in own]
        t_cw1 = [Q.dma("S", own[kv].take(), own[kv].ap, A["cw1"][:, kv, :], own[kv].sem) for kv in range(2)]
        CT = Ring([Buf(attnT[:, q, :]) for q in range(4)])
        getG = ftiles(A["mgg"], 16)
        t_gt = []

        def gates(g):
            for n in range(4 * g, 4 * g + 4):
                pb, t = yield from proj_steps(getG, n, 16)
                t = act([t, own[n % 2].free], GT[n % 2][:, n // 2, :], pb.ap, ACT.Tanh, scale=0.5)
                pb.free = [t]
                t_gt.append(t)
                yield


        lru = X.rearrange("p a b -> p (a b)")[:, 0:2048].rearrange("p (a b c) -> p a b c", a=2, b=8)
        tW = Q.dma("S", [t_xn], lru, A["lru"], s_lru)
        cw = sm("cw")

        def gelu2(src, w, dst):
            b1, w1 = TMP.take()
            t = act([w, w1], b1.ap, src, ACT.Square)
            t = ts("V", [t], b1.ap, b1.ap, 0.044715, 1.0, ALU.mult, ALU.add)
            t = tt("V", [t], b1.ap, b1.ap, src, ALU.mult)
            t = act([t], b1.ap, b1.ap, ACT.Tanh, scale=math.sqrt(2.0 / math.pi))
            t = stt([t], dst, b1.ap, 1.0, src, ALU.add, ALU.mult)
            b1.free = [t]
            return t

        t_gr = []
        t_rnn = []

        def recurrent():
            for half in range(2):
                t_T, t_G = [], []
                conv = {}
                for q in range(5):
                    if q < 4:
                        m = 4 * half + q
                        pb, t = yield from proj_steps(getF, 10 + 8 * half + q, 26)
                        xr, w = XR.take()
                        tz = Q.memset("G", w, xr.ap[:, 0:3], 0.0)
                        t = cp("A", [t, w], xr.ap[:, 3:515], pb.ap)
                        pb.free = [t]
                        xc, w = XC.take()
                        t = ts("V", [t, tz, w, t_c], xc.ap, xr.ap[:, 0:512], cw[:, m:m + 1], sm("cb")[:, m:m + 1], ALU.mult, ALU.add)
                        for j in range(1, 4):
                            t = stt([t], xc.ap, xr.ap[:, j:j + 512], cw[:, 8 * j + m:8 * j + m + 1], xc.ap, ALU.mult, ALU.add)
                        xr.free = [t]
                        conv[q] = (xc, t)
                        yield
                        if q == 1:
                            yield from gates(2 * half)
                    if q == 0:
                        continue
                    m = 4 * half + q - 1
                    xc, tx = conv[q - 1]
                    for which in range(2):
                        b, bw = dense.take()
                        t = mm([tW, tx, bw], b.ap, lru[:, which, m, :], xc.ap, True, True, sig=True)
                        tmp, w = TMP.take()
                        ta = act([t, w, t_hb], tmp.ap, b.ap, ACT.Tanh, scale=0.5, bias=halfb[:, 8 * which + m:8 * which + m + 1])
                        b.free = [ta]
                        if which == 0:
                            t = act([ta, t_sp, xn_read, t_rnn[-1:]], T_[:, q - 1, :], tmp.ap, ACT.Tanh,
                                    scale=m2sp[:, m:m + 1], bias=m2sp[:, m:m + 1])
                            t_T.append(t)
                        else:
                            t = stt([ta, t_rnn[-1:], xn_read], GX[:, q - 1, :], tmp.ap, 1.0, xc.ap, ALU.add, ALU.mult)
                            xc.free = [t]
                            t_G.append(t)
                        tmp.free = [t]
                        yield
                for q in range(4):
                    m = 4 * half + q
                    pb, t = yield from proj_steps(getF, 14 + 8 * half + q, 26)
                    t = gelu2(pb.ap, [t], GR[:, m, :])
                    pb.free = [t]
                    t_gr.append(t)
                    yield
                    Tm, Gm = T_[:, q, :], GX[:, q, :]
                    sq, w = TMP.take()
                    ta = act([t_T, w], sq.ap, Tm, ACT.Sqrt, scale=-1.0)
                    rc, w = TMP.take()
                    t = ts("V", [t_T, w], rc.ap, Tm, -1.0, 1.0, ALU.mult, ALU.add)
                    t = rcp([t], rc.ap, rc.ap)
                    yield
                    t1 = stt([t, ta], Tm, Tm, 1.0, rc.ap, ALU.add, ALU.mult)
                    t = tt("V", [t1, ta], sq.ap, sq.ap, rc.ap, ALU.mult)
                    t = tt("V", [t, t_G], Gm, Gm, sq.ap, ALU.mult)
                    sq.free = [t]
                    yield
                    t = Q.scan([t], rc.ap, Tm, Gm)
                    t = stt([t, t_gr], GR[:, m, :], rc.ap, 0.5, GR[:, m, :], ALU.mult, ALU.mult)
                    rc.free = [t]
                    t_rnn.append(t)
                    if q == 1:
                        yield from gates(2 * half + 1)
                    yield

        def compress():
            res = []
            cring = Ring(banks[6:8])
            for kv in range(2):
                b, tw = own[kv], t_cw1[kv]
                w1 = view(b.ap, 0, 16, 256)
                pos = sm("pk" if kv == 0 else "pv")
                tb = []
                blk = BLK[kv].rearrange("p t (g n) -> p t g n", g=2)
                for g in range(2):
                    v = KC[kv][:, g, :].rearrange("p (n b two) -> p b n two", b=8, two=2)
                    for a in range(2):
                        tb.append(tt("V", [t_kc[kv], t_c], blk[:, 8 * a:8 * a + 8, g, :], v[:, :, a:a + 31, 0],
                                     bc(pos[:, 8 * a:8 * a + 8], 2, 31), ALU.add))
                yield 1
                hid, hw = CT.take()
                hid4 = view(hid.ap, 0, 2, 62)
                th = []
                for ht in range(2):
                    pb, bw = cring.take()
                    for k in range(16):
                        t = mm([tw, tb, bw], pb.ap[:, 0:62], w1[:, k, 128 * ht:128 * ht + 128], BLK[kv][:, k, :], k == 0, k == 15, sig=k == 15)
                    src = pb.ap[:, 0:62]
                    u, uw = CT.take()
                    ua = u.ap[:, 0:62]
                    t0 = t
                    t = act([t, uw], ua, src, ACT.Square)
                    t = ts("V", [t], ua, ua, 0.044715, 1.0, ALU.mult, ALU.add)
                    t = tt("V", [t], ua, ua, src, ALU.mult)
                    t = act([t], ua, ua, ACT.Tanh, scale=math.sqrt(2.0 / math.pi))
                    t = ts("V", [t], ua, ua, 1.0, 0.5, ALU.add, ALU.mult)
                    t = tt("V", [t, hw], hid4[:, ht, :], ua, src, ALU.mult)
                    u.free = [t]
                    pb.free = [t]
                    th.append(t)
                b.free = [t0]
                yield 3
                w2 = sm("kw2" if kv == 0 else "vw2").rearrange("p (a b) -> p a b", a=2)
                pb, bw = cring.take()
                if kv == 0:
                    for g in range(2):
                        for ht in range(2):
                            t = mm([th, bw, t_c], pb.ap[64 * g:64 * g + 64, 0:31], w2[:, ht, :], hid4[:, ht, 31 * g:31 * g + 31],
                                   ht == 0, ht == 1, sig=ht == 1)
                    kcT = small(31)
                    res.append(kcT)
                    tk = cp("V", [t], kcT, pb.ap[:, 0:31])
                else:
                    for g in range(2):
                        for ht in range(2):
                            t = mm([th, bw, t_c], pb.ap[0:31, 64 * g:64 * g + 64], hid4[:, ht, 31 * g:31 * g + 31], w2[:, ht, :],
                                   ht == 0, ht == 1, sig=ht == 1)
                    vc = small(128)
                    res.append(vc)
                    tk = cp("V", [t], vc[0:31, :], pb.ap[0:31, 0:128])
                pb.free = [tk]
                hid.free = [t]
                res.append(tk)
                yield 3
            cmpres.extend(res)

        cmpres = []
        t_attn = []
        attn_banks = banks[2:8]
        t_pct = []

        def cmp_scores():
            kcT, tkc, vc, tvc = cmpres
            for i in range(4):
                for h in range(2):
                    pb, bw = attn_banks[h], attn_banks[h].take()
                    ps3 = pb.ap[:, 0:124].rearrange("p (j n) -> p j n", j=4)
                    for j in range(4):
                        t = mm([tkc, t_q, bw], ps3[:, j, :], qT[64 * h:64 * h + 64, j, 128 * i:128 * i + 128],
                               kcT[64 * h:64 * h + 64, :], True, True, sig=j == 3)
                    sb, sw = CT.take()
                    s3 = view(sb.ap, 0, 4, 31)
                    st = view(sb.ap, 124, 4, 1)[:, :, 0]
                    t = tt("V", [t, sw, t_c], s3, ps3, bc(ck("cneg")[:, 31 * i:31 * i + 31], 1, 4), ALU.add)
                    pb.free = [t]
                    t = red([t], st, s3, ALU.max)
                    t = tt("V", [t], s3, s3, bc(st, 2, 31), ALU.subtract)
                    t = act([t], s3, s3, ACT.Exp, scale=0.125)
                    t = tt("V", [t], s3, s3, bc(ck("c01")[:, 31 * i:31 * i + 31], 1, 4), ALU.mult)
                    t = red([t], st, s3, ALU.add)
                    t = ts("V", [t], st, st, 1e-20, None, ALU.max)
                    t = rcp([t], st, st)
                    gcol = gate[:, i, :].rearrange("p (hd c) -> p hd c", c=3)[:, 4 * h:4 * h + 4, 0]
                    t = tt("V", [t, t_gate], st, st, gcol, ALU.mult)
                    t = tt("V", [t], s3, s3, bc(st, 2, 31), ALU.mult)
                    yield 2
                    p2, p2w = attn_banks[2 + h], attn_banks[2 + h].take()
                    for j in range(4):
                        t2 = tr([t, p2w], p2.ap[0:31, 128 * j:128 * j + 128], s3[:, j, :], ident, sig=j == 3)
                    sb.free = [t2]
                    t = cp("AV"[h], [t2, t_blk], PCT[0:31, 4 * h:4 * h + 4, 128 * i:128 * i + 128],
                           p2.ap[0:31, :].rearrange("p (a b) -> p a b", a=4))
                    p2.free = [t]
                    t_pct.append(t)

        def attention():
            kcT, tkc, vc, tvc = cmpres
            SPs = [Buf(PS[:, 1024:2048].rearrange("p (a b) -> p a b", a=2)), Buf(PS[:, 2048:3072].rearrange("p (a b) -> p a b", a=2))]
            SPs[0].free = attn_banks[0].take() + attn_banks[1].take()
            SPs[1].free = attn_banks[2].take() + attn_banks[3].take()
            PTb, Ob = attn_banks[4], attn_banks[5]
            n = 0
            o_free = Ob.take()
            ct_free = [b.free for b in CT.bufs]
            units = [(j, i, h) for j in range(4) for i in range(4) for h in range(2)]

            def scores(n):
                j, i, h = units[n]
                nk = 128 * (i + 1)
                hd = 4 * h + j
                S = SPs[n % 2]
                sw = S.take()
                hs = slice(64 * h, 64 * h + 64)
                for ty in range(2):
                    mm([t_q, t_k, sw], S.ap[:, ty, 0:nk], qT[hs, j, 128 * i:128 * i + 128], kT[hs, ty, 0:nk], True, False)
                    t = mm([t_c], S.ap[:, ty, nk - 128:nk], ident, ck("neg"), False, True, sig=True)
                st = ST[n % 2]
                mx, rs = st.ap[:, 0:2], st.ap[:, 2:4]
                pr = PR[n % 2]
                pw = pr.take()
                t = red([t, st.take()], mx, S.ap[:, :, 0:nk], ALU.max)
                t = ts("V", [t], mx, mx, -0.125, None, ALU.mult)
                te = None
                for ty in range(2):
                    te = act([t, pw], pr.ap[:, ty, 0:nk], S.ap[:, ty, 0:nk], ACT.Exp, bias=mx[:, ty:ty + 1], scale=0.125,
                             acc=rs[:, ty:ty + 1])
                S.free = [te]
                yield 1
                t = ts("V", [te], rs, rs, 1e-20, None, ALU.max)
                t = rcp([t], rs, rs)
                t = tt("V", [t, t_gate], rs, rs, gate[:, i, 3 * hd + 1:3 * hd + 3], ALU.mult)
                dg = DG[n % 2]
                dw = dg.take()
                for ty in range(2):
                    td = ts("V", [t, dw], dg.ap[:, ty, :], ident, rs[:, ty:ty + 1], None, ALU.mult)
                st.free = [td]
                return pr, dg, te, td

            nxt = yield from scores(0)
            o_toks = []
            for n, (j, i, h) in enumerate(units):
                nk = 128 * (i + 1)
                hd = 4 * h + j
                hs = slice(64 * h, 64 * h + 64)
                pr, dg, te, td = nxt
                if n + 1 < len(units):
                    nxt = yield from scores(n + 1)
                for ty in range(2):
                    ptw = PTb.take()
                    for kb in range(i + 1):
                        t = mm([te, td, ptw], PTb.ap[:, 128 * kb:128 * kb + 128], pr.ap[:, ty, 128 * kb:128 * kb + 128],
                               dg.ap[:, ty, :], True, True, sig=kb == i)
                    pt, ptsw = PTR.take()
                    tp = cp("AV"[ty], [t, ptsw], pt.ap[:, 0:nk], PTb.ap[:, 0:nk])
                    PTb.free = [tp]
                    if ty == 1:
                        pr.free = [t]
                        dg.free = [t]
                    yield 1
                    for kb in range(i + 1):
                        t = mm([tp, t_v, o_free], Ob.ap[hs, 128 * i:128 * i + 128],
                               Vn[:, kb, 128 * ty + 64 * h:128 * ty + 64 * h + 64], pt.ap[:, 128 * kb:128 * kb + 128],
                               ty == 0 and kb == 0, False, sig=kb == i)
                    pt.free = [t]
                t = mm([tvc, t_pct], Ob.ap[hs, 128 * i:128 * i + 128], vc[0:31, 64 * h:64 * h + 64], PCT[0:31, hd, 128 * i:128 * i + 128],
                       False, True, sig=True)
                o_toks.append(t)
                yield 1
                if i == 3 and h == 1:
                    t = cp("V", [o_toks, ct_free], attnT[:, j, :], Ob.ap)
                    o_free = [t]
                    o_toks = []
                    t_attn.append(t)
            Ob.free = o_free
            attn_banks[0].free = attn_banks[1].free = SPs[0].free
            attn_banks[2].free = attn_banks[3].free = SPs[1].free

        ST = [Buf(small(4)) for _ in range(2)]
        DG = [Buf(zal(2, 128)) for _ in range(2)]

        def attention_branch():
            yield from compress()
            t_blk.extend([cmpres[1], cmpres[3]])
            yield from cmp_scores()
            yield from attention()

        t_blk = []
        weave(attention_branch(), recurrent())

        allb = Ring(banks)
        t_x = Q.dma("A", [t_rnn], X, A["x"].rearrange("(i p) d -> p i d", p=P), s_x)
        MG = XN

        def products_of(slot, pieces, w, pr):
            b, tw = slot
            return [ftile(pr, lambda k, off=off: b.ap[:, off + 128 * k:off + 128 * k + 128], rhs, nk, [tw, w]) for off, rhs, nk in pieces]

        def merge(pbs, dst, w, tmp):
            out_t = []
            half = []
            for g in range(2):
                x, xw = tmp.take()
                pg, tg = pbs[g]
                py, ty = pbs[2 + g]
                t = act([tg, xw], x.ap, pg.ap, ACT.Tanh, scale=0.5)
                pg.free = [t]
                t = stt([t, ty], x.ap, x.ap, 1.0, py.ap, ALU.add, ALU.mult)
                py.free = [t]
                half.append((x, t))
            t = tt("V", [half[0][1], half[1][1], w], dst, half[0][0].ap, half[1][0].ap, ALU.add)
            half[0][0].free = [t]
            half[1][0].free = [t]
            return t

        t_mg = []
        for m in range(8):
            if m % 2 == 0:
                b, tw = weights(A["mgy"][:, 3072 * (m // 2):3072 * (m // 2) + 3072], 3072)
            o = 1536 * (m % 2)
            pa, ta = ftile(allb, lambda k: b.ap[:, o + 128 * k:o + 128 * k + 128], lambda k: attnT[:, k, :], 4, [tw, t_attn])
            pr_, tr_ = ftile(allb, lambda k: b.ap[:, o + 512 + 128 * k:o + 640 + 128 * k], lambda k: GR[:, k, :], 8, [tw, t_rnn])
            if m % 2:
                b.free = [tr_]
            g0, g1 = GT[0][:, m, :], GT[1][:, m, :]
            t0 = stt([ta, t_gt], g0, g0, 1.0, pa.ap, ALU.add, ALU.mult)
            pa.free = [t0]
            t1 = stt([tr_], g1, g1, 1.0, pr_.ap, ALU.add, ALU.mult)
            pr_.free = [t1]
            t_mg.append(tt("G", [t0, t1, t_rnn], MG[:, m // 2, 512 * (m % 2):512 * (m % 2) + 512], g0, g1, ALU.add))
        for b in own:
            b.free = [t_mg[-1]]
        WQ = Ring([WR[1], WR[2], WR[0], WR[3]])

        def residual(src, MGk, w):
            t_r = []
            tl = None
            for nh in range(2):
                b, tw = weights(src[:, 4096 * nh:4096 * nh + 4096])
                w_ = view(b.ap, 0, 8, 512)
                for i in range(4):
                    pb, bw = allb.take()
                    for k in range(8):
                        t = mm([tw, w, bw], pb.ap, MGk(k)[:, 128 * i:128 * i + 128], w_[:, k, :], k == 0, k == 7, sig=k == 7)
                    tl = t
                    xs = X[:, i, 512 * nh:512 * nh + 512]
                    t = stt([t, t_x], xs, pb.ap, 0.5, xs, ALU.mult, ALU.add)
                    pb.free = [t]
                    t_r.append(t)
                b.free = [tl]
            return t_r, tl

        t_x1, t_last = residual(A["wo1"], lambda k: MG[:, k // 2, 512 * (k % 2):512 * (k % 2) + 512], t_mg)

        H4 = H.rearrange("p a b -> p (a b)").rearrange("p (a b) -> p a b", b=1024)
        t_xn = normed(X, [[t_x1[4 + i], t_mg] for i in range(4)], XN, w_out=t_last, scratch=H4)
        t_h = transposed(XN, [t_xn], H, sm("n2"), allb, [t_last])
        HT = view(zone, 4096, 32, 512)
        b0, b1_ = 0, 20480
        PB = view(zone, b0, 2, 32, 8)
        PC = view(zone, b0 + 512, 2, 32, 8)
        BB = view(zone, b0 + 1024, 2, 32, 16)
        CC = view(zone, b0 + 2048, 2, 32, 16)
        sat = [b0 + 3072]

        def s32(*shape):
            n = 1
            for d in shape:
                n *= d
            a = view(zone, sat[0], *shape)
            sat[0] += n
            assert sat[0] <= b0 + 4096
            return a

        nC = s32(512)
        BZ = view(zone, b1_, 4, 512)
        T1 = view(zone, b1_ + 2048, 512)
        T2 = view(zone, b1_ + 2560, 512)
        Mr = view(zone, b1_ + 3072, 512)
        Mi = view(zone, b1_ + 3584, 512)
        Zt = view(zone, b1_ + 4096, 1088)
        pslot = WR[3]
        WQ = Ring([WR[1], WR[2], WR[0]])
        MB2 = [view(pslot.ap, 1024 * q, 2, 512) for q in range(2)]
        TD2 = [view(pslot.ap, 2048 + 1024 * q, 2, 512) for q in range(2)]
        keep = ck("neg")
        U8 = keep[:, 0:64].rearrange("p (a b) -> p a b", a=2)
        RHO8 = keep[:, 64:96]
        cm_tmp = ck("cneg")[:, 0:124]
        s_bc = sem("s_bc")

        def cmul(out, x, y, w):
            a = cm_tmp[:, 0:64].rearrange("p (a b) -> p a b", a=2)
            b = ck("c01")[:, 0:64].rearrange("p (a b) -> p a b", a=2)
            t1 = tt("V", w, a, x, bc(y[:, 0, :], 1, 2), ALU.mult)
            t2 = tt("V", w, b, x, bc(y[:, 1, :], 1, 2), ALU.mult)
            t = tt("V", [t1, t2], out[:, 0, :], a[:, 0, :], b[:, 1, :], ALU.subtract)
            return tt("V", [t], out[:, 1, :], a[:, 1, :], b[:, 0, :], ALU.add)

        def wide_exp(x, w):
            a, b = s32(32), s32(32)
            t = act(w, a, x, ACT.Tanh, scale=1.0 / 16)
            t = ts("V", [t], b, a, -1.0, 1.0, ALU.mult, ALU.add)
            t = rcp([t], b, b)
            t = stt([t], a, a, 1.0, b, ALU.add, ALU.mult)
            for _ in range(3):
                t = tt("V", [t], a, a, a, ALU.mult)
            return a, t

        t_store = []
        ssm_state = {}

        def ssm_prep(w0, pr):
            w0 = [w0, t_c]
            t_bb = Q.dma("A", w0, BB.rearrange("p a b c -> p (a b c)"), A["bb"], s_bc)
            t_bb = Q.dma("A", w0, CC.rearrange("p a b c -> p (a b c)"), A["cc"], s_bc)
            dt, t = wide_exp(sm("ldt"), w0)
            x = s32(32)
            t = tt("V", [t], x, sm("are"), dt, ALU.mult)
            th = dt
            t = tt("V", [t], th, sm("aim"), dt, ALU.mult)
            ea, t = wide_exp(x, [t])
            k = x
            t = ts("V", [t], k, th, 1.0 / (2 * math.pi), 12582912.0, ALU.mult, ALU.add)
            t = ts("V", [t], k, k, 12582912.0, None, ALU.subtract)
            t = stt([t], th, k, -6.28125, th, ALU.mult, ALU.add)
            t = stt([t], th, k, -(2 * math.pi - 6.28125), th, ALU.mult, ALU.add)
            t = ts("V", [t], th, th, 3.1415925, -3.1415925, ALU.min, ALU.max)
            yield
            u = s32(2, 32)
            a1 = s32(2, 32)
            ta = act([t], u[:, 1, :], th, ACT.Sin)
            ta = act([t], u[:, 0, :], th, ACT.Sin, scale=0.5)
            t = tt("V", [ta], u[:, 0, :], u[:, 0, :], u[:, 0, :], ALU.mult)
            t = ts("V", [t], u[:, 0, :], u[:, 0, :], -2.0, 1.0, ALU.mult, ALU.add)
            t = tt("V", [t], a1, u, bc(ea, 1, 2), ALU.mult)
            t_a = t
            t = tt("V", [t], ea, ea, ea, ALU.mult)
            t = tt("V", [t], ea, ea, ea, ALU.mult)
            t = tt("V", [t], RHO8, ea, ea, ALU.mult)
            t = cmul(U8, u, u, [t])
            t = cmul(u, U8, U8, [t])
            t = cmul(U8, u, u, [t])
            ssm_state["t"] = t
            yield
            cur = [s32(2, 32), s32(2, 32)]
            g = Q.memset("V", [t], cur[0][:, 0, :], 1.0)
            t = Q.memset("V", [g], cur[0][:, 1, :], 0.0)
            tg = None
            rel = [None, None]
            for j in range(9):
                c = cur[j % 2]
                lo, hi = slice(0, 64), slice(64, 128)
                if j < 8:
                    tg = cp("V", [t], PB[lo, :, :, 7 - j], c[lo])
                    tg = cp("V", [t], PB[hi, :, :, j], c[hi])
                if j > 0:
                    tg = cp("V", [t], PC[lo, :, :, j - 1], c[lo])
                    tg = cp("V", [t], PC[hi, :, :, 8 - j], c[hi])
                rel[j % 2] = tg
                if j < 8:
                    t = cmul(cur[1 - j % 2], c, a1, [t, rel[1 - j % 2], t_a])
                if j % 3 == 2:
                    yield
            t_pw = tg
            lr, li = sm("are"), sm("aim")
            am = cur[1]
            t = ts("V", [t, t_pw], am[:, 0, :], a1[:, 0, :], -1.0, None, ALU.add)
            f = u
            q_, r_ = th, ea
            t = tt("V", [t], q_, lr, lr, ALU.mult)
            t = tt("V", [t], r_, li, li, ALU.mult)
            t = tt("V", [t], q_, q_, r_, ALU.add)
            t = rcp([t], q_, q_)
            t = tt("V", [t], f[:, 0, :], am[:, 0, :], lr, ALU.mult)
            t = tt("V", [t], r_, a1[:, 1, :], li, ALU.mult)
            t = tt("V", [t], f[:, 0, :], f[:, 0, :], r_, ALU.add)
            t = tt("V", [t], f[:, 1, :], a1[:, 1, :], lr, ALU.mult)
            t = tt("V", [t], r_, am[:, 0, :], li, ALU.mult)
            t = tt("V", [t], f[:, 1, :], f[:, 1, :], r_, ALU.subtract)
            t = tt("V", [t], f, f, bc(q_, 1, 2), ALU.mult)
            yield
            v = lambda a: a.rearrange("p (a b) -> p a b", a=32)
            fr, fi = bc(f[:, 0, :], 2, 16), bc(f[:, 1, :], 2, 16)
            w = [t, t_bb]
            t1 = tt("V", w, v(T1), BB[:, 0], fr, ALU.mult)
            t2 = tt("V", w, v(T2), BB[:, 1], fi, ALU.mult)
            t3 = tt("V", w, v(Mr), BB[:, 0], fi, ALU.mult)
            t4 = tt("V", w, v(Mi), BB[:, 1], fr, ALU.mult)
            t = tt("V", [t1, t2, t3, t4], BB[:, 0], v(T1), v(T2), ALU.subtract)
            t = tt("V", [t], BB[:, 1], v(Mr), v(Mi), ALU.add)
            tz = Q.memset("G", w0, BZ, 0.0)
            flat = BB.rearrange("p a b c -> p a (b c)")
            t_bz = []
            for ri in range(2):
                t_bz.append(cp("V", [t, tz], BZ[0:64, ri, :], flat[0:64, ri, :]))
                t_bz.append(cp("V", [t, tz], BZ[64:128, 2 + ri, :], flat[64:128, ri, :]))
            t_nc = ts("V", [t_bb, t_bz[-1]], nC, CC[:, 1].rearrange("p a b -> p (a b)"), -1.0, None, ALU.mult)
            t_pw = [t_pw, t_nc]
            yield
            s_sts = [sem("s_sta"), sem("s_stb")]
            c4 = lambda a: a.rearrange("p (a b c) -> p a b c", a=4, b=8)
            zd = A["z_d"]
            start = [t_nc, t_pw, pslot.take()]

            def outer(pwt, mat, c, mr, mi, neg, w):
                gs = slice(4 * c, 4 * c + 4)
                p0, p1 = bc(pwt[:, 0, gs, :], 3, 16), bc(pwt[:, 1, gs, :], 3, 16)
                m0, m1 = bc(mat[:, 0, gs, :], 2, 8), bc(mat[:, 1, gs, :], 2, 8)
                t1 = tt("V", w, c4(T1), p0, m0, ALU.mult)
                t2 = tt("G", w, c4(T2), p1, m1, ALU.mult)
                ta = tt("V", [t1, t2, w], mr, T1, T2, ALU.subtract)
                t1 = tt("V", [ta], c4(T1), p0, m1, ALU.mult)
                t2 = tt("G", [ta], c4(T2), p1, m0, ALU.mult)
                if neg:
                    t1 = tt("V", [t1, t2], mi, T1, T2, ALU.add)
                    return ts("V", [t1], mi, mi, -1.0, None, ALU.mult)
                return tt("V", [t1, t2], mi, T1, T2, ALU.add)

            tr_free = [start]
            mb_free = [[start], [start]]
            td_free = [[], []]
            Z_free = []

            def products(c, w):
                ta = outer(PB, BB, c, Mr, Mi, False, [tr_free, w])
                mb = MB2[c % 2]
                return ta, outer(PC, CC, c, mb[:, 0, :], mb[:, 1, :], True, [ta, mb_free[c % 2]])

            nxt = products(0, [])
            yield
            for c in range(8):
                gs = slice(4 * c, 4 * c + 4)
                s_st = s_sts[c % 2]
                ta, tb = nxt
                pb, bw = pr.take()
                pb2_, bw2 = pr.take()
                for q in range(4):
                    tr([ta, bw, t_c], pb.ap[:, 128 * q:128 * q + 128], Mr[:, 128 * q:128 * q + 128], ident)
                for q in range(4):
                    tp = tr([bw2], pb2_.ap[:, 128 * q:128 * q + 128], Mi[:, 128 * q:128 * q + 128], ident, sig=q == 3)
                td = TD2[c % 2]
                t1 = cp("A", [tp, start, td_free[c % 2]], td[:, 0, :], pb.ap)
                t2 = cp("A", [tp], td[:, 1, :], pb2_.ap)
                pb.free = [t1]
                pb2_.free = [t2]
                tr_free = [tp]
                Q.dma("A", [t1], mbr_d[:, gs, :], td[:, 0, :].rearrange("p (a b) -> p a b", a=4), s_st)
                d1 = Q.dma("A", [t2], mbi_d[:, gs, :], td[:, 1, :].rearrange("p (a b) -> p a b", a=4), s_st)
                mb = MB2[c % 2]
                Q.dma("A", [tb], mcr_d[:, gs, :], mb[:, 0, :].rearrange("p (a b) -> p a b", a=4), s_st)
                d2 = Q.dma("A", [tb], mci_d[:, gs, :], mb[:, 1, :].rearrange("p (a b) -> p a b", a=4), s_st)
                if c < 7:
                    nxt = products(c + 1, [tb])
                yield
                zt = []
                for q in range(4):
                    gg = 4 * c + q
                    pb, bw = pr.take()
                    cols = slice(16 * gg, 16 * gg + 16)
                    mm_ = (mb[:, 0, 128 * q:128 * q + 128], mb[:, 1, 128 * q:128 * q + 128])
                    for at0, n, zr, ri_, rhs in (
                            (0, 128, BZ[:, 2, cols], BZ[:, 3, cols], mm_),
                            (128, 16, flat[:, 0, cols], flat[:, 1, cols], (CC[:, 0, gg, :], nC[:, cols])),
                            (144, 128, BZ[:, 0, cols], BZ[:, 1, cols], mm_)):
                        mm([tb, bw, t_nc], pb.ap[0:16, at0:at0 + n], zr, rhs[0], True, False)
                        tp = mm([], pb.ap[0:16, at0:at0 + n], ri_, rhs[1], False, True, sig=at0 == 144)
                    t1 = cp("A", [tp, Z_free], Zt[0:16, 272 * q:272 * q + 272], pb.ap[0:16, 0:272])
                    pb.free = [t1]
                    zt.append(t1)
                    if q == 1:
                        yield
                d3 = Q.dma("A", zt, zd[:, gs, :], Zt[0:16, :].rearrange("p (a b) -> p a b", a=4), s_st)
                Z_free = [d3]
                td_free[c % 2] = [d3]
                mb_free[c % 2] = [tp, d3]
                yield
            pslot.free = [d3, tp]
            t_store.extend(td_free)

        def weights_from(src, w):
            b, w2 = WQ.take()
            if isinstance(src, str):
                for ji in range(8):
                    t = Q.dma("S", [w, w2], b.ap[16 * ji:16 * ji + 16, :].rearrange("p (a b) -> p a b", a=32),
                              A["z_d"][:, :, 16 * (8 - ji):16 * (8 - ji) + 128], b.sem)
                return b, t
            t = Q.dma("S", [w, w2], b.ap, src.rearrange("p a b -> p (a b)"), b.sem)
            return b, t

        A["z_d"] = dram("z_d", (16, 32, 272))
        getM = ftiles(A["m1"], 32)
        t_m = []

        def mlp_in():
            for m in range(32):
                pb, t = proj(getM, m, hk, t_h, allb, 32)
                t = act([t], HT[:, m, :], pb.ap, ACT.Relu)
                pb.free = [t]
                t_m.append(tt("G", [t], HT[:, m, :], HT[:, m, :], HT[:, m, :], ALU.mult))
                yield 1

        weave(mlp_in(), ssm_prep([t_h], allb))
        t_ssm = ssm_state["t"]
        Ep = view(zone, 20480, 2, 32, 64)
        te = Q.memset("G", [t_store, t_m[-1]], Ep[:, 0, :, 0], 1.0)
        te = Q.memset("G", [te], Ep[:, 1, :, 0], 0.0)
        pw = U8
        tpw = t_ssm
        pb2 = [view(zone, 2048 + 64 * q, 2, 32) for q in range(2)]
        big = view(zone, 0, 2048)
        for q in range(6):
            n = 1 << q
            ta = bc(pw[:, 0, :], 2, n)
            tb = bc(pw[:, 1, :], 2, n)
            er, ei = Ep[:, 0, :, 0:n], Ep[:, 1, :, 0:n]
            o_r, o_i = Ep[:, 0, :, n:2 * n], Ep[:, 1, :, n:2 * n]
            tm = view(big, 0, 32, 64)[:, :, 0:n]
            w = [te, tpw]
            t = tt("V", w, o_r, er, ta, ALU.mult)
            t1 = tt("V", w, tm, ei, tb, ALU.mult)
            t = tt("V", [t, t1], o_r, o_r, tm, ALU.subtract)
            t2 = tt("V", [t], o_i, er, tb, ALU.mult)
            t1 = tt("V", [t], tm, ei, ta, ALU.mult)
            te = tt("V", [t1, t2], o_i, o_i, tm, ALU.add)
            if q < 5:
                nx = pb2[q % 2]
                tpw = cmul(nx, pw, pw, [tpw, te])
                pw = nx
        t_E = te
        bw = [b.take() for b in banks]
        for s_ in range(8):
            b, tw = weights(A["m2"][:, 4096 * s_:4096 * s_ + 4096])
            w_ = view(b.ap, 0, 4, 1024)
            for q in range(4):
                k = 4 * s_ + q
                for i in range(4):
                    for nh in range(2):
                        t = mm([tw, t_m[k], bw[2 * i + nh]], banks[2 * i + nh].ap, HT[:, k, 128 * i:128 * i + 128],
                               w_[:, q, 512 * nh:512 * nh + 512], k == 0, k == 31, sig=(k == 31 or (q == 3 and i == 3 and nh == 1)))
                        if k == 31:
                            xs = X[:, i, 512 * nh:512 * nh + 512]
                            banks[2 * i + nh].free = [tt("V", [t], xs, xs, banks[2 * i + nh].ap, ALU.add)]
            b.free = [t]
        t_x2 = [b.free[0] for b in banks]

        row = view(zone, 24576, 1024)

        def rowload(name, w, s):
            return Q.dma("A", w, row, A[name].partition_broadcast(P), s)

        s_row = sem("s_row")
        zfree = [t_x2, t_store, t_E]
        t_row = rowload("fn1", zfree, s_row)
        t_xb = normed(X, [[t_x2[2 * i:2 * i + 2], t_E] for i in range(4)], XN, None, row, t_row, X)
        t_x = t_xb
        t_row = rowload("gf", [t_xb], s_row)
        s_rw = sem("s_rw")
        Q.dma("A", [], RW, A["rw"], s_rw)
        t_rw = Q.dma("A", [], RB, A["rb"].partition_broadcast(P), s_rw)
        t_xn = normed(X, t_xb, XN)
        t_h = transposed(XN, [t_xn], H, sm("mix"), allb, [])

        Vp = view(zone, 0, 2, 32, 64)
        tmpA = view(zone, 4096, 2, 32, 64)
        ufT = view(zone, 12288, 4, 512)
        RHO = view(zone, 8192, 32, 64)
        usT = view(zone, 10240, 4, 512)
        yfT = view(zone, 12288, 4, 512)
        U = view(zone, 14336, 32, 64)
        Sp = view(zone, 16384, 2, 32, 64)

        vslot = WQ.bufs[WQ.i]
        WQ = Ring([b for b in [WR[3]] + WQ.bufs[WQ.i:] + WQ.bufs[:WQ.i] if b is not vslot])
        Vf = view(vslot.ap, 0, 4, 4, 256)
        vslot_free = vslot.take()
        getZ = ftiles(A["z2"], 8)
        t_uf, t_us = [], []
        for m in range(4):
            pb, t = proj(getZ, m, hk, t_h, allb, 8)
            dst = usT[:, m, :].rearrange("p (j k) -> p j k", j=8)
            pb.free = [cp("AV"[m % 2], [t], dst, pb.ap.rearrange("p (k j) -> p j k", j=8))]
            t_us += pb.free
        s_u = sem("s_u")
        t_ud = Q.dma("A", [t_us], u_d.rearrange("(m p) t -> p m t", p=P), usT, s_u)
        s_u2 = sem("s_u2")
        uv = u_d.rearrange("(g c) (j k) -> j c g k", c=16, j=8)
        for j in range(8):
            t_U = Q.dma("A", [t_ud], U[16 * j:16 * j + 16, :, :], uv[j], s_u2)

        for m in range(4):
            pb, t = proj(getZ, 4 + m, hk, t_h, allb, 8)
            pb.free = [cp("AV"[m % 2], [t, t_xb], ufT[:, m, :], pb.ap)]
            t_uf += pb.free
        bF, tF = weights(A["dft"])

        t_rho = cp("V", [t_x2, t_ssm], RHO, bc(RHO8, 2, 64))
        t_rho = Q.memset("V", [t_rho], RHO[:, :, 0], 0.0)

        WQ = Ring(WQ.bufs[WQ.i:] + WQ.bufs[:WQ.i])
        t_V = []
        for ri, src in ((0, mbr_d), (1, mbi_d)):
            b, tw = weights_from(src, t_store)
            w_ = view(b.ap, 0, 32, 128)
            for g8 in range(4):
                pb, bw = allb.take()
                for q in range(8):
                    g = 8 * g8 + q
                    t = mm([tw, t_U, bw], pb.ap[:, 64 * q:64 * q + 64], w_[:, g, :], U[:, g, :], True, True, sig=q == 7)
                src3 = pb.ap.rearrange("p (a b) -> p a b", a=8)
                dst = Vp[:, ri, 8 * g8:8 * g8 + 8, :]
                ta = cp("A", [t], dst[0:64], src3[0:64])
                tb = cp("V", [t], dst[64:128], src3[64:128, :, ::-1])
                pb.free = [ta, tb]
                t_V += [ta, tb]
            b.free = [t]
        WQ.i = 0
        vr, vi, er, ei = Vp[:, 0], Vp[:, 1], Ep[:, 0], Ep[:, 1]
        ar, ai = tmpA[:, 0], tmpA[:, 1]
        w = [t_V, t_E, t_rho]
        gr_, gi_ = Sp[:, 0], Sp[:, 1]
        t1 = tt("V", w, ar, vr, er, ALU.mult)
        t2 = tt("V", w, ai, vi, ei, ALU.mult)
        t3 = tt("V", w, gr_, vi, er, ALU.mult)
        t4 = tt("V", w, gi_, vr, ei, ALU.mult)
        t5 = tt("V", [t1, t2, t4], vr, ar, ai, ALU.add)
        t6 = tt("V", [t3, t4, t5], vi, gr_, gi_, ALU.subtract)

        def fl(a):
            return a.rearrange("p a b -> p (a b)")
        t7 = Q.scan([t5, t6], fl(ar), fl(RHO), fl(vr))
        t8 = Q.scan([t6, t7], fl(ai), fl(RHO), fl(vi))
        t1 = tt("V", [t7], vr, ar, er, ALU.mult)
        t2 = tt("V", [t8], vi, ai, ei, ALU.mult)
        tz = Q.memset("G", [t6], Sp[0:64, :, :, 0], 0.0)
        tz = Q.memset("G", [t6, tz], Sp[64:128, :, :, 63], 0.0)
        t_S = []
        f_, b_ = slice(0, 64), slice(64, 128)
        t_S.append(tt("V", [t1, t2, tz, t6], gr_[f_, :, 1:64], vr[f_, :, 0:63], vi[f_, :, 0:63], ALU.subtract))
        t_S.append(tt("V", [t1, t2, tz], gr_[b_, :, 62::-1], vr[b_, :, 0:63], vi[b_, :, 0:63], ALU.subtract))
        t1 = tt("V", [t_S], vr, ar, ei, ALU.mult)
        t2 = tt("V", [t_S], vi, ai, er, ALU.mult)
        t_S.append(tt("V", [t1, t2, tz], gi_[f_, :, 1:64], vr[f_, :, 0:63], vi[f_, :, 0:63], ALU.add))
        t_S.append(tt("V", [t1, t2, tz], gi_[b_, :, 62::-1], vr[b_, :, 0:63], vi[b_, :, 0:63], ALU.add))

        slots = [weights_from("z", t_store)]

        def half_load(hf, b):
            w = b.take()
            for n, src in enumerate((mcr_d, mci_d)):
                t = Q.dma("S", [w, t_store], b.ap[:, 2048 * n:2048 * n + 2048], src[:, 16 * hf:16 * hf + 16, :].rearrange("p a b -> p (a b)"), b.sem)
            slots.append((b, t))

        half_load(0, WQ.bufs[1])
        cf = view(bF.ap, 0, 2, 4, 512)
        t_vf = []
        for i in range(4):
            for gp in range(2):
                pb, bw = allb.take()
                for q in range(2):
                    t = mm([t_uf, bw, t_c], pb.ap[:, 256 * q:256 * q + 256], ufT[:, 2 * gp + q, 128 * i:128 * i + 128], ck("cs"),
                           True, True, sig=q == 1)
                pb.free = [cp("A", [t, vslot_free], Vf[:, i, 2 * gp:2 * gp + 2, :], pb.ap.rearrange("p (a b) -> p a b", a=2))]
                t_vf += pb.free
        t_yf = []
        for g in range(4):
            pb, bw = allb.take()
            for k in range(8):
                t = mm([t_vf, tF, bw], pb.ap, Vf[:, k % 4, g, 128 * (k // 4):128 * (k // 4) + 128], cf[:, k // 4, k % 4, :], k == 0, k == 7, sig=k == 7)
            pb.free = [cp("A", [t, t_vf], yfT[:, g, :], pb.ap)]
            t_yf += pb.free
        bF.free = [t]
        vslot.free = [t]
        half_load(1, bF)
        WQ = Ring([vslot] + WQ.bufs)
        YS = view(zone, 4096, 32, 64)
        t_y = []
        for g8 in range(4):
            pb, bw = allb.take()
            for q in range(8):
                g = 8 * g8 + q
                for k, rhs in enumerate((U[:, g, :], Sp[:, 0, g, :], Sp[:, 1, g, :])):
                    b, tw = slots[0] if k == 0 else slots[1 + g // 16]
                    o = 128 * g if k == 0 else 2048 * (k - 1) + 128 * (g % 16)
                    t = mm([tw, t_S, bw, t_U], pb.ap[:, 64 * q:64 * q + 64], b.ap[:, o:o + 128], rhs, k == 0, k == 2, sig=k == 2 and q == 7)
            pb.free = [cp("AV"[g8 % 2], [t, t_S], YS[:, 8 * g8:8 * g8 + 8, :], pb.ap.rearrange("p (a b) -> p a b", a=8))]
            t_y += pb.free
        for b, _ in slots:
            b.free = [t]

        def begin(m, pr):
            slot = weights(A["mg2"][:, 3072 * m:3072 * m + 3072], 3072)
            return slot, products_of(slot, [(0, hk, 8), (1024, hk, 8), (2048, lambda k: yfT[:, k, :], 4)], [t_h, t_yf], pr)

        early = [begin(m, Ring(banks[3 * m:3 * m + 3])) for m in range(2)]
        glu_banks = Ring(banks[6:8])
        s_y1 = sem("s_y1")
        s_y2 = sem("s_y2")
        yv = yo_d.rearrange("(g c) (j k) -> j c g k", c=16, j=8)
        for j in range(8):
            t_yd = Q.dma("A", [t_y], yv[j], YS[16 * j:16 * j + 16, :, :], s_y1)
        yT = view(zone, 0, 4, 512)
        yG = view(zone, 2048, 4, 512)
        t_yl = Q.dma("A", [t_yd, t_S], yT, yo_d.rearrange("(m p) t -> p m t", p=P), s_y2)
        TM2 = Ring([Buf(view(zone, 6144 + 512 * q, 512)) for q in range(4)])
        t_g = []
        for m in range(4):
            b1, w1 = TM2.take()
            y = yT[:, m, :]
            t = stt([t_yl, t_c, t_y], y, usT[:, m, :], sm("dsk")[:, m:m + 1], y, ALU.mult, ALU.add)
            t = act([t, w1], b1.ap, y, ACT.Square)
            t = ts("V", [t], b1.ap, b1.ap, 0.044715, 1.0, ALU.mult, ALU.add)
            t = tt("V", [t], b1.ap, b1.ap, y, ALU.mult)
            t = act([t], b1.ap, b1.ap, ACT.Tanh, scale=math.sqrt(2.0 / math.pi))
            t = ts("V", [t], b1.ap, b1.ap, 1.0, 0.5, ALU.add, ALU.mult)
            t = tt("V", [t], y, b1.ap, y, ALU.mult)
            b1.free = [t]
            t_g.append(t)
        bG, tG = weights(A["glu"], 2048)
        wg_ = view(bG.ap, 0, 4, 4, 128)
        t_ys = []
        for m in range(4):
            pb, t = ftile(glu_banks, lambda k: wg_[:, m, k, :], lambda k: yT[:, k, :], 4, [tG, t_g])
            b1, w1 = TM2.take()
            t_gl = t
            t = act([t, w1], b1.ap, pb.ap, ACT.Tanh, scale=0.5)
            pb.free = [t]
            t = ts("V", [t], b1.ap, b1.ap, 1.0, 0.5, ALU.add, ALU.mult)
            t = tt("V", [t], yG[:, m, :].rearrange("p (k j) -> p j k", j=8), b1.ap.rearrange("p (j k) -> p j k", j=8),
                   yT[:, m, :].rearrange("p (j k) -> p j k", j=8), ALU.mult)
            b1.free = [t]
            t_ys.append(t)
        bG.free = [t_gl]

        MG = view(zone, 16384, 8, 512)
        t_mg = []
        for m in range(8):
            slot, pbs = early.pop(0) if early else begin(m, allb)
            pbs += products_of(slot, [(2560, lambda k: yG[:, k, :], 4)], [t_ys], allb if m > 1 else glu_banks)
            slot[0].free = [pbs[-1][1]]
            t_mg.append(merge(pbs, MG[:, m, :], [t_S, t_y], TM2))
        t_x3, t_last = residual(A["wo2"], lambda k: MG[:, k, :], t_mg)

        XN = view(zone, 0, 4, 1024)
        t_hn = normed(X, [[t_x3[4 + i], t_mg] for i in range(4)], XN, None, row, t_row, XN)
        s_hn = sem("s_hn")
        t_hnd = Q.dma("A", [t_hn], hn_d.rearrange("(i p) d -> p i d", p=P), XN, s_hn)
        t_h = transposed(XN, [t_hn], H, None, allb, [t_last])
        rw = RW.rearrange("p (a b) -> p a b", a=8)
        z = [4096]

        def zl(*shape):
            n = 1
            for d in shape:
                n *= d
            a = view(zone, z[0], *shape)
            z[0] += n
            return a

        LG = zl(4, 72)
        pb, bw = allb.take()
        for i in range(4):
            for k in range(8):
                t = mm([t_h, bw, t_rw], pb.ap[:, 72 * i:72 * i + 72], H[:, k, 128 * i:128 * i + 128], rw[:, k, :], k == 0, k == 7, sig=k == 7)
        t = tt("V", [t, t_last, t_rw], LG, pb.ap[:, 0:288].rearrange("p (a b) -> p a b", a=4), bc(RB, 1, 4), ALU.add)
        pb.free = [t]
        t_lg = t
        mx8 = zl(4, 8)
        ix8 = zl(4, 8)
        for i in range(4):
            t = Q.add("V", [t_lg], lambda eng, i=i: eng.max(mx8[:, i, :], LG[:, i, 0:8]))
            t = Q.add("V", [t], lambda eng, i=i: eng.max_index(ix8.bitcast(U32)[:, i, :], mx8[:, i, :], LG[:, i, 0:8]))
        gi = zl(4)
        t = cp("V", [t], gi, ix8.bitcast(U32)[:, :, 0])
        pg = zl(4)
        e8 = zl(4, 8)
        ta = tt("V", [t], e8, LG[:, :, 0:8], bc(mx8[:, :, 0], 2, 8), ALU.subtract)
        ta = act([ta], e8, e8, ACT.Exp)
        ta = red([ta], pg, e8, ALU.add)
        t_pg = rcp([ta], pg, pg)
        oh = zl(4, 8)
        t = tt("V", [t_pg], oh, bc(ck("iota")[:, 0:8], 1, 4), bc(gi, 2, 8), ALU.is_equal)
        le = zl(4, 8, 8)
        for i in range(4):
            t = tt("V", [t], le[:, i, :, :], LG[:, i, 8:72].rearrange("p (g e) -> p g e", g=8), bc(oh[:, i, :], 2, 8), ALU.mult)
        es = zl(4, 8)
        for i in range(4):
            t = red([t], es[:, i, :], le[:, i, :, :].rearrange("p g e -> p e g"), ALU.add)
        m2 = zl(4, 8)
        i2 = zl(4, 8)
        for i in range(4):
            t = Q.add("V", [t], lambda eng, i=i: eng.max(m2[:, i, :], es[:, i, :]))
            t = Q.add("V", [t], lambda eng, i=i: eng.max_index(i2.bitcast(U32)[:, i, :], m2[:, i, :], es[:, i, :]))
        EX = zl(2, 4)
        WT = zl(2, 4)
        for c in range(2):
            t = cp("V", [t], EX[:, c, :], i2.bitcast(U32)[:, :, c])
            t = stt([t], EX[:, c, :], gi, 8.0, EX[:, c, :], ALU.mult, ALU.add)
        e1 = zl(4)
        t = tt("V", [t], e1, m2[:, :, 1], m2[:, :, 0], ALU.subtract)
        t = act([t], e1, e1, ACT.Exp)
        dn = zl(4)
        t = ts("V", [t], dn, e1, 1.0, None, ALU.add)
        t = rcp([t], dn, dn)
        t = tt("V", [t], WT[:, 0, :], dn, pg, ALU.mult)
        t = tt("V", [t], WT[:, 1, :], WT[:, 0, :], e1, ALU.mult)
        E = zl(2, 4, 64)
        for c in range(2):
            t = tt("V", [t], E[:, c, :, :], bc(ck("iota")[:, 0:64], 1, 4), bc(EX[:, c, :], 2, 64), ALU.is_equal)
        ES = zl(4, 64)
        t = tt("V", [t], ES, E[:, 0, :, :], E[:, 1, :, :], ALU.add)
        pb, bw = allb.take()
        for i in range(4):
            for j in range(i + 1):
                tp = mm([t, bw], pb.ap[:, 64 * i:64 * i + 64], ck("tri") if j == i else ck("ones"), ES[:, j, :], j == 0, j == i)
        for j in range(4):
            tp = mm([], pb.ap[:, 256:320], ck("ones"), ES[:, j, :], j == 0, j == 3, sig=j == 3)
        RK = zl(2, 4)
        rt = zl(4, 64)
        for c in range(2):
            t = tt("V", [tp, t], rt, E[:, c, :, :], pb.ap[:, 0:256].rearrange("p (a b) -> p a b", a=4), ALU.mult)
            t = red([t], RK[:, c, :], rt, ALU.add)
        cnt = zl(1)
        t = red([t], cnt, pb.ap[:, 256:320], ALU.max)
        pb.free = [t]
        NR = zl(1).bitcast(I32)
        sh = CAP.bit_length() - 1
        t = ts("V", [t], cnt, cnt, float(CAP - 1), None, ALU.add)
        t = cp("V", [t], NR, cnt)
        t_nr = ts("V", [t], NR, NR, sh, None, ALU.logical_shift_right)
        EI = zl(2, 4).bitcast(I32)
        HI = zl(2, 4)
        LO = zl(2, 4)
        tI = zl(2, 4).bitcast(I32)
        t = cp("V", [t_nr], EI, EX)
        t = ts("V", [t], tI, EI, 1, None, ALU.logical_shift_right)
        t = cp("V", [t], HI, tI)
        t = ts("V", [t], tI, EI, 1, None, ALU.bitwise_and)
        t = cp("V", [t], LO, tI)
        t = ts("V", [t], LO, LO, 64.0, None, ALU.mult)
        t_route = t

        RR = zl(2, 4)
        OK = zl(2, 4)
        o2 = zl(2, 4)
        SLf = zl(2, 4)
        SL = zl(2, 4).bitcast(I32)
        TABr = zl(32)
        TAB = TABr.bitcast(I32)
        WR_ = zl(2, 4)
        OFF = zl(1)
        IDX = zl(1).bitcast(I32)
        XGb = [Buf(zl(1024)) for _ in range(2)]
        xt0 = z[0]
        XTb = [Buf(zl(8, 128)) for _ in range(2)]
        ATb = Buf(zl(512))
        aTb = Buf(zl(4, 128))
        YEb = Buf(zl(1024))
        YGb = XGb
        AM = view(zone, xt0, 2, 4, 128)
        BM = view(zone, xt0 + 1024, 2, 4, 32)
        ring0 = z[0]
        nring = (24576 - ring0) // 4096
        t_off = Q.memset("V", [t_route], OFF, 0.0)

        def plan(Q, w, bank):
            t = Q.ts("V", w, RR, RK, OFF, None, ALU.subtract)
            t = Q.ts("V", [t], OK, RR, 0.0, None, ALU.is_ge)
            t = Q.ts("V", [t], o2, RR, float(CAP), None, ALU.is_lt)
            t = Q.tt("V", [t], OK, OK, o2, ALU.mult)
            t = Q.tt("V", [t], RR, RR, OK, ALU.mult)
            t = Q.tt("V", [t], WR_, WT, OK, ALU.mult)
            t = Q.stt([t], SLf, EX, 64.0, RR, ALU.mult, ALU.add)
            t_sl = Q.cp("V", [t], SL, SLf)
            t = Q.tt("V", [t_sl], o2, LO, RR, ALU.add)
            for c in range(2):
                t = Q.tt("V", [t], AM[:, c, :, :], bc(ck("iota"), 1, 4), bc(o2[:, c, :], 2, 128), ALU.is_equal)
                t = Q.tt("V", [t], BM[:, c, :, :], bc(ck("iota")[:, 0:32], 1, 4), bc(HI[:, c, :], 2, 32), ALU.is_equal)
            t = Q.tt("V", [t], OK, OK, bc(ck("tok"), 1, 2), ALU.mult)
            for c in range(2):
                t = Q.tt("V", [t], BM[:, c, :, :], BM[:, c, :, :], bc(OK[:, c, :], 2, 32), ALU.mult)
            for n in range(8):
                tp = Q.mm([t, w], bank.ap[:, 0:32], AM[:, n // 4, n % 4, :], BM[:, n // 4, n % 4, :], n == 0, n == 7, sig=n == 7)
            t_tab = Q.cp("V", [tp], TAB, bank.ap[:, 0:32])
            return t_tab, t_sl, t

        def expert_pair(Q, q, idx, w_idx, wsrc, wload, mb, xg, xt, at_, aT, ye, gsem, ysem, y_out, tw_extra=()):
            g, gw = xg, xg.take()
            tg = Q.gather([gw, w_idx], g.ap, hn_d, idx, gsem)
            x, xw = xt, xt.take()
            tx = []
            for hf in range(2):
                b, bw = mb.take()
                for k in range(4):
                    kk = 4 * hf + k
                    t = Q.tr([tg, bw], b.ap[:, 128 * k:128 * k + 128], g.ap.rearrange("p (a b) -> p b a", b=8)[:, kk, :], ident, sig=k == 3)
                t2 = Q.cp("AV"[hf], [t, xw], x.ap[:, 4 * hf:4 * hf + 4, :], b.ap.rearrange("p (a b) -> p a b", a=4))
                b.free = [t2]
                tx.append(t2)
            g.free = [t]
            res = []
            for mat in range(2):
                s0, w0 = wload(mat, 0)
                s1, w1 = wload(mat, 1)
                pb, bw = mb.take()
                for k in range(8):
                    for e in range(2):
                        s, w_ = ((s0, w0), (s1, w1))[e]
                        t = Q.mm([tx, w_, bw], pb.ap[64 * e:64 * e + 64, :], x.ap[:, k, 64 * e:64 * e + 64], s.ap[:, 512 * k:512 * k + 512],
                                 k == 0, k == 7, sig=k == 7)
                s0.free = [t]
                s1.free = [t]
                res.append((pb, t))
            x.free = [t]
            a, aw = at_, at_.take()
            (pg_, tg_), (pu_, tu_) = res
            t = Q.act([tg_, aw], a.ap, pg_.ap, ACT.Tanh, scale=0.5)
            t = Q.stt([t], a.ap, a.ap, 1.0, pg_.ap, ALU.add, ALU.mult)
            pg_.free = [t]
            t = Q.stt([t, tu_], a.ap, a.ap, 0.5, pu_.ap, ALU.mult, ALU.mult)
            pu_.free = [t]
            b, bw = mb.take()
            for k in range(4):
                tt_ = Q.tr([t, bw], b.ap[:, 128 * k:128 * k + 128], a.ap.rearrange("p (a b) -> p b a", b=4)[:, k, :], ident, sig=k == 3)
            a.free = [tt_]
            c, cw_ = aT, aT.take()
            t_a = Q.cp("A", [tt_, cw_], c.ap, b.ap.rearrange("p (a b) -> p a b", a=4))
            b.free = [t_a]
            s0, w0 = wload(2, 0)
            s1, w1 = wload(2, 1)
            y, yw = ye, ye.take()
            ty = []
            for nh in range(2):
                pb, bw = mb.take()
                for k in range(4):
                    for e in range(2):
                        s, w_ = ((s0, w0), (s1, w1))[e]
                        t = Q.mm([t_a, w_, bw], pb.ap[64 * e:64 * e + 64, :], c.ap[:, k, 64 * e:64 * e + 64],
                                 s.ap[:, 1024 * k + 512 * nh:1024 * k + 512 * nh + 512], k == 0, k == 3, sig=k == 3)
                t2 = Q.cp("VA"[nh], [t, yw], y.ap[:, 512 * nh:512 * nh + 512], pb.ap)
                pb.free = [t2]
                ty.append(t2)
            s0.free = [t]
            s1.free = [t]
            c.free = [t]
            td = Q.dma("A", ty, y_out, y.ap, ysem)
            y.free = [td]
            return td

        def combine(Q, w, gsems, bufs):
            out_t = []
            for n in range(8):
                i, c = n // 2, n % 2
                b = bufs[n % len(bufs)]
                t = Q.gather([w, b.take()], b.ap, y_d, SL[:, c, i:i + 1], gsems[n % len(bufs)])
                t = Q.stt([t] + out_t[-1:], X[:, i, :], b.ap, WR_[:, c, i:i + 1], X[:, i, :], ALU.mult, ALU.add)
                b.free = [t]
                out_t.append(t)
            return out_t

        t_tab, t_sl, t_pl = plan(Q, [t_off, t_last, t_h, allb.bufs[0].free], allb.bufs[0])
        allb.bufs[0].free = [t_tab]

        gsem = [sem("s_ga"), sem("s_gb")]
        ysem = [sem("s_ya"), sem("s_yb")]
        csem = [sem(f"s_c{n}") for n in range(8)]
        extra = [Buf(view(zone, ring0 + 4096 * q, 4096), sem(f"wx{q}")) for q in range(nring)]
        for b in extra:
            b.free = [t_last]
        extra += [Buf(view(zone, 0, 4096), sem("wxn")), Buf(H.rearrange("p a b -> p (a b)"), sem("wh"))]
        extra[-2].free = [t_h, t_hnd]
        extra[-1].free = [t_lg]
        assert z[0] <= ring0
        start = WQ.i
        MQ = Ring(WR[start:] + WR[:start] + extra)

        EW = [A["eg"].rearrange("e (p t) n -> e p (t n)", p=P), A["eu"].rearrange("e (p t) n -> e p (t n)", p=P),
              A["ed"].rearrange("e (p t) n -> e p (t n)", p=P)]
        mb = Ring(banks)
        ends = []
        for q in range(32):
            def wload(mat, e, q=q):
                b, w = MQ.take()
                return b, Q.dma("S", w, b.ap, EW[mat][2 * q + e], b.sem)
            ends.append(expert_pair(Q, q, TAB[:, q:q + 1], [t_tab, t_hnd], None, wload, mb, XGb[q % 2], XTb[q % 2], ATb, aTb, YEb,
                                    gsem[q % 2], ysem[q % 2], y_d[128 * q:128 * q + 128, :]))
        YGm = [Buf(view(zone, ring0 + 1024 * n, 1024)) for n in range(8)]
        for b in YGm:
            b.free = extra[0].free + extra[1].free
        t_cb = combine(Q, [ends], csem, YGm)

        Z = view(zone, 0, 4, 1024)
        v_, s4, r4 = (view(zone, 4096 + 4 * n, 4) for n in range(3))

        def last_rstd(Q, w, w_z):
            t = None
            for i in range(4):
                t = Q.act([w[i], w_z, t], Z[:, i, :], X[:, i, :], ACT.Square, acc=v_[:, i:i + 1])
            t = Q.ts("V", [t], v_, v_, 1.0 / 1024, 1e-6, ALU.mult, ALU.add)
            t = Q.act([t], s4, v_, ACT.Sqrt)
            t = Q.rcp([t], r4, s4)
            t = Q.tt("V", [t], s4, r4, r4, ALU.mult)
            t = Q.tt("V", [t], s4, s4, v_, ALU.mult)
            t = Q.ts("V", [t], s4, s4, -0.5, 1.5, ALU.mult, ALU.add)
            return Q.tt("V", [t], r4, r4, s4, ALU.mult)

        t_cb.append(last_rstd(Q, [t_cb[2 * i + 1] for i in range(4)], [extra[-2].free, t_h, t_lg]))

        r_sems = {e: sem("r" + e) for e in "TVAG"}
        r_dma = [sem(f"r_d{q}") for q in range(6)]
        r_g = sem("r_g")
        r_y = sem("r_y")
        r_c = [sem("r_ca"), sem("r_cb")]
        meet_in = sem("meet")
        go = {e: sem("go" + e) for e in "TVAG"}
        clear = list(r_sems.values()) + r_dma + [r_g, r_y] + r_c

        def part(build):
            q2 = Queue(r_sems)
            for b in banks + XGb + XTb + [ATb, aTb, YEb] + WR + extra:
                b.free = []
            build(q2)
            for e in "TVAG":
                n = q2.n.get(r_sems[e].name, 0)
                if n:
                    q2.wait(e, [(r_sems[e], n)])
            gathers = [(s, q2.n[s.name]) for s in [r_g] + r_c if q2.n.get(s.name, 0)]
            if gathers:
                q2.wait("G", gathers)
                q2.raw("G", lambda eng: eng.dma_reset())
            return q2

        def more(q2):
            t = q2.ts("V", [], OFF, OFF, float(CAP), None, ALU.add)
            plan(q2, [t], banks[0])

        def pair_part(q2, reg):
            def wload(mat, e):
                n = 2 * mat + e
                b = (WR + extra)[n]
                w = b.take()
                d = r_dma[n]

                def go_(eng):
                    eng.dma_start(b.ap, EW[mat][bass.ds(reg["S"] * 2 + e, 1), :, :].rearrange("a p f -> p (a f)")).then_inc(d, 16)
                q2.wait("S", w)
                q2.n[d.name] = 16
                q2.raw("S", go_)
                return b, (d, 16)
            t = q2.add("V", [], lambda eng: eng.tensor_copy(IDX, TAB[:, bass.ds(reg["V"], 1)]))

            def st(eng):
                eng.dma_start(y_d.rearrange("(q p) d -> q p d", p=P)[bass.ds(reg["A"], 1), :, :].rearrange("a p d -> p (a d)"), YEb.ap).then_inc(r_y, 16)
            expert_pair_dyn(q2, t, wload, st)

        def expert_pair_dyn(q2, t_idx, wload, st):
            orig = q2.dma

            def dma(e, w, out, in_, sem_):
                q2.wait(e, w)
                q2.n[sem_.name] = q2.n.get(sem_.name, 0) + 16
                q2.raw(e, st)
                return (sem_, q2.n[sem_.name])
            q2.dma = dma
            t = expert_pair(q2, 0, IDX, [t_idx], None, wload, Ring(banks), XGb[0], XTb[0], ATb, aTb, YEb, r_g, r_y, None)
            q2.dma = orig
            q2.wait("A", [t])

        def tail(q2):
            ends2 = combine(q2, [], r_c, YGb)
            last_rstd(q2, [ends2[2 * i + 1] for i in range(4)], [])

        reg = {}
        P_more = part(more)
        P_pair = part(lambda q2: pair_part(q2, reg))
        P_tail = part(tail)

        s_fin = sem("s_fin")
        t_row = Q.dma("A", [t_hn], row, A["fn2"].partition_broadcast(P), s_row)

        QF = Queue({e: sem("f" + e) for e in "TVAG"})

        def last_norm():
            td = []
            for i in range(4):
                t1 = QF.stt([], Z[:, i, :], X[:, i, :], r4[:, i:i + 1], row, ALU.mult, ALU.mult)
                td.append(QF.dma("S", [t1], out[128 * i:128 * i + 128, :], Z[:, i, :], s_fin))
            QF.wait("S", td[-1:])

        last_norm()

        def meet(eng, e, first=False):
            if e == "S":
                eng.wait_ge(meet_in, 4)
                eng.sem_clear(meet_in)
                for s in clear:
                    eng.sem_clear(s)
                for k in "TVAG":
                    eng.sem_inc(go[k], 1)
            else:
                eng.sem_inc(meet_in, 1)
                eng.wait_ge(go[e], 1)
                eng.sem_clear(go[e])

        Q.wait("V", [t_cb])
        Q.wait("A", [t_row, ends])
        for e in "TVAGS":
            Q.wait(e, [t_nr])
            if e != "V":
                Q.wait(e, [t_cb[-1]])
        with nc.Block() as block:
            for e, on in (("S", block.sync), ("T", block.tensor), ("V", block.vector), ("A", block.scalar), ("G", block.gpsimd)):
                @on
                def _(eng, e=e):
                    for f in Q.q[e]:
                        f(eng)
                    rounds = eng.value_load(NR[0:1, 0:1], min_val=1, max_val=512 // CAP)
                    r = eng.alloc_register("round" + e)
                    eng.reg_mov(r, 1)
                    meet(eng, e)
                    with eng.While(lambda: eng.snap(r) < rounds):
                        for f in P_more.q[e]:
                            f(eng)
                        meet(eng, e)
                        k = eng.alloc_register("pair" + e)
                        eng.reg_mov(k, 0)
                        with eng.While(lambda: eng.snap(k) < 32):
                            reg[e] = eng.snap(k, min_val=0, max_val=31)
                            for f in P_pair.q[e]:
                                f(eng)
                            meet(eng, e)
                            eng.reg_add(k, k, 1)
                        for f in P_tail.q[e]:
                            f(eng)
                        meet(eng, e)
                        eng.reg_add(r, r, 1)
                    for f in QF.q[e]:
                        f(eng)


def host(inp):
    g = {k: np.asarray(v) for k, v in inp.items()}
    w = g["w_in"][0]
    off = np.cumsum([0, 512, 128, 128, 128, 128, 128, 128, 24, 1024, 1024, 1024, 1024])
    cols = []
    for j in range(4):
        cols += [np.arange(64 * j, 64 * j + 64), np.arange(64 * (j + 4), 64 * (j + 4) + 64)]
    cols += [np.arange(off[3], off[3] + 128), np.arange(off[5], off[5] + 128)]
    for b in (off[1], off[2]):
        for q in range(2):
            cols += [np.arange(b + 64 * q, b + 64 * q + 64)] * 2
    for half in range(2):
        for b in (off[8], off[9]):
            cols += [np.arange(b + 512 * half, b + 512 * half + 512)]
    cols = np.concatenate(cols)

    def ft(a):
        K, M = a.shape
        return np.ascontiguousarray(a.reshape(K // 128, 128, M // 128, 128).transpose(1, 2, 0, 3))

    def rows(a):
        K, N = a.shape
        return np.ascontiguousarray(a.reshape(K // 128, 128, N).transpose(1, 0, 2).reshape(128, -1))

    def halves(a):
        return np.concatenate([rows(a[:, :512]), rows(a[:, 512:])], 1)

    def pf(a):
        return a.reshape(-1, 128).T

    o = {"x": g["x"][0]}
    o["winF"] = ft(w[:, cols]).reshape(128, -1)
    o["winN"] = rows(w[:, np.concatenate([np.arange(off[4], off[4] + 128), np.arange(off[6], off[6] + 128), np.arange(off[7], off[7] + 24)])])
    heads = np.concatenate([np.arange(64 * hd, 64 * hd + 64) for j in range(4) for hd in (j, j + 4)])
    o["mgg"] = np.concatenate([ft(w[:, off[10]:off[11]]).reshape(128, 8, -1), ft(w[:, off[11]:off[12]]).reshape(128, 8, -1)],
                              2).reshape(128, -1)
    o["mgy"] = np.concatenate([ft(g["w_up_attn"][0][heads]).reshape(128, 8, -1), ft(g["w_up_rnn"][0]).reshape(128, 8, -1)],
                              2).reshape(128, -1)
    o["wo1"] = halves(g["w_out"][0])
    o["m1"] = ft(g["mlp_w1"][0]).reshape(128, -1)
    o["m2"] = rows(g["mlp_w2"][0])
    lru = np.zeros((128, 2, 8, 128), np.float32)
    for q, n in enumerate(("lru_w_a", "lru_w_i")):
        a = g[n][0].reshape(8, 2, 64, 64)
        for b in range(2):
            lru[64 * b:64 * b + 64, q, :, 64 * b:64 * b + 64] = a[:, b].transpose(1, 0, 2)
    o["lru"] = lru
    o["cw1"] = np.stack([rows(g["cmp_k_w1"][0]), rows(g["cmp_v_w1"][0])], 1)
    sm = np.zeros((128, SM_N), np.float32)

    def put(n, a):
        c, k = SM_COLS[n]
        sm[:, c:c + k] = a.reshape(128, k)

    put("n1", pf(g["norm1_w"]))
    put("n2", pf(g["norm2_w"]))
    put("mix", pf(g["mix_norm_g_2"]))
    put("cw", np.concatenate([pf(g["conv_w"][0][i]) for i in range(4)], 1))
    put("cb", pf(g["conv_b"]))
    put("ba", pf(g["lru_b_a"]))
    put("bi", pf(g["lru_b_i"]))
    put("lam", pf(g["lru_lambda"]))
    put("dsk", pf(g["ssm_D_2"]))
    put("are", g["ssm_A_re_2"][0].transpose(0, 2, 1))
    put("aim", g["ssm_A_im_2"][0].transpose(0, 2, 1))
    put("ldt", np.repeat(g["ssm_log_dt_2"][0][:, None, :], 64, 1))
    put("pk", g["cmp_pos_k"][0].reshape(16, 128).T)
    put("pv", g["cmp_pos_v"][0].reshape(16, 128).T)
    put("kw2", g["cmp_k_w2"][0].reshape(2, 128, 64).transpose(1, 0, 2))
    put("vw2", g["cmp_v_w2"][0].reshape(2, 128, 64).transpose(1, 0, 2))
    o["sm"] = sm
    ckc = np.zeros((128, CK_N), np.float32)

    def putc(n, a):
        c, k = CK_COLS[n]
        ckc[:, c:c + k] = a.reshape(128, k)

    r = np.arange(128)
    putc("ident", np.eye(128))
    putc("neg", np.where(r[None, :] > r[:, None], -1e30, 0.0))
    tq = r[:, None] + 128 * np.arange(4)[None, :]
    ok = (16 * np.arange(31) + 31)[None, None, :] <= tq[:, :, None]
    putc("cneg", np.where(ok, 0.0, -1e30))
    putc("c01", np.where(ok, 1.0, 0.0))
    putc("tri", (r[:, None] < r[None, :]).astype(np.float32))
    putc("ones", np.ones((128, 128)))
    putc("iota", np.tile(r[None, :], (128, 1)))
    putc("tok", tq)
    ang = 2 * np.pi * (np.outer(r, r) % 128) / 128
    putc("cs", np.concatenate([np.cos(ang), np.sin(ang)], 1) / 256)
    o["ck"] = ckc
    o["fn1"], o["gf"], o["fn2"] = g["final_norm_w"], g["ffn_norm_g_2"][0], g["final_norm_g_2"]

    def nb(a):
        return a.reshape(128, 512)

    o["bb"] = np.concatenate([nb(g["ssm_B_%s_2" % n][0].transpose(0, 2, 1, 3)) for n in ("re", "im")], 1)
    o["cc"] = np.concatenate([nb(g["ssm_C_%s_2" % n][0].transpose(0, 3, 1, 2)) for n in ("re", "im")], 1)
    w2 = g["w_in_2"][0]
    o["z2"] = ft(np.concatenate([w2[:, 512:1024], w2[:, :512]], 1)).reshape(128, -1)
    o["mg2"] = np.concatenate([ft(w2[:, 1024:2048]).reshape(128, 8, -1), ft(w2[:, 2048:]).reshape(128, 8, -1),
                               ft(g["w_fourier_out_2"][0]).reshape(128, 8, -1), ft(g["w_ssm_out_2"][0]).reshape(128, 8, -1)], 2).reshape(128, -1)
    o["wo2"] = halves(g["w_out_2"][0])
    o["glu"] = ft(g["ssm_w_glu_2"][0]).reshape(128, -1)
    n = np.arange(512)
    a5 = 2 * np.pi * (np.outer(n, n) % 512) / 512
    o["dft"] = np.concatenate([rows(np.cos(a5)), rows(-np.sin(a5))], 1).astype(np.float32)
    o["eg"], o["eu"], o["ed"] = (g["expert_w_%s_2" % n][0] for n in ("gate", "up", "down"))
    o["rw"] = rows(np.concatenate([g["router_group_w_2"][0], g["router_expert_w_2"][0]], 1))
    o["rb"] = np.concatenate([g["router_group_b_2"][0], g["router_expert_b_2"][0]])
    return {k: np.ascontiguousarray(v) for k, v in o.items()}


_INS = ["x", "sm", "ck", "rw", "rb", "winF", "winN", "lru", "cw1", "mgg", "mgy", "wo1", "m1", "m2", "fn1", "bb", "cc", "z2", "dft", "glu",
        "mg2", "wo2", "gf", "fn2", "eg", "eu", "ed"]


def kernel(**inputs):
    import concourse.bacc as bacc
    from concourse.bass_utils import run_bass_kernel_spmd

    arrays = host(inputs)
    nc = bacc.Bacc("TRN2", target_bir_lowering=False, num_devices=1)
    A = {n: nc.dram_tensor("in_" + n, arrays[n].shape, F32, kind="ExternalInput").ap() for n in _INS}
    out = nc.dram_tensor("out_0", (512, 1024), F32, kind="ExternalOutput").ap()
    program(nc, A, out)
    r = run_bass_kernel_spmd(nc, [{"in_" + n: arrays[n] for n in _INS}], core_ids=[0])
    return r.results[0]["out_0"].reshape(1, 512, 1024)
```
